# Optimizing a Trainium2 kernel written in Bass

```python
import jax, jax.numpy as jnp
from jax import lax
import numpy as np
import math

D_MODEL = 1024
BATCH = 1
SEQ = 512
DEPTH = 1

CHUNK = 64
N_META = 16
EPS = 1e-6
POOL_WIDTH = 512
POOL_GROUPS = 4
POOL_GROUP_DIM = POOL_WIDTH // POOL_GROUPS
POOL_WINDOWS = (2, 4, 8, 16)
GLA_HEADS = 4
GLA_DK = 64
GLA_DV = 128
GLA_KEY = GLA_HEADS * GLA_DK
GLA_VAL = GLA_HEADS * GLA_DV
GLA_GATE_RANK = 16
GLA_TAU = 16.0
D_FF = 4 * D_MODEL
IN_SIZES = (POOL_WIDTH, GLA_KEY, GLA_KEY, GLA_VAL, GLA_VAL, GLA_GATE_RANK, D_MODEL, D_MODEL)
N_IN = sum(IN_SIZES)
IN_SPLITS = [int(s) for s in np.cumsum(IN_SIZES)[:-1]]


def rmsnorm(x, g):
    xf = x.astype(jnp.float32)
    y = xf * lax.rsqrt(jnp.mean(xf * xf, axis=-1, keepdims=True) + EPS)
    return (y * g.astype(jnp.float32)).astype(x.dtype)

def multiscale_pool(a):
    B, L, _ = a.shape
    af = a.astype(jnp.float32)
    cs = jnp.concatenate([jnp.zeros((B, 1, POOL_WIDTH), jnp.float32), jnp.cumsum(af, axis=1)], axis=1)
    t = jnp.arange(L)
    outs = []
    for g, w in enumerate(POOL_WINDOWS):
        lo_c, hi_c = g * POOL_GROUP_DIM, (g + 1) * POOL_GROUP_DIM
        hi = cs[:, 1:, lo_c:hi_c]
        lo = jnp.concatenate([jnp.zeros((B, w - 1, POOL_GROUP_DIM), jnp.float32), cs[:, :L - w + 1, lo_c:hi_c]], axis=1)
        cnt = jnp.minimum(t + 1, w).astype(jnp.float32)[None, :, None]
        outs.append((hi - lo) / cnt)
    return (jnp.concatenate(outs, axis=-1) - af).astype(a.dtype)

def gla_chunk_step(S, inp):
    qc, kc, vc, ac = inp
    b = jnp.cumsum(ac, axis=2)
    decay = jnp.exp(-jnp.abs(b[:, :, :, None, :] - b[:, :, None, :, :]))
    scores = jnp.einsum('bhtk,bhsk,bhtsk->bhts', qc, kc, decay)
    o = jnp.einsum('bhts,bhsv->bhtv', scores, vc) + jnp.einsum('bhtk,bhkv->bhtv', qc * jnp.exp(b), S)
    b_end = b[:, :, -1:, :]
    S_new = jnp.exp(b_end[:, :, 0, :])[..., None] * S + jnp.einsum('bhsk,bhsv->bhkv', kc * jnp.exp(b_end - b), vc)
    return S_new, o

def gla_chunked(q, k, v, log_a):
    B = q.shape[0]
    pad = CHUNK - N_META

    def prep(t):
        t = jnp.pad(t.astype(jnp.float32), ((0, 0), (pad, 0), (0, 0), (0, 0)))
        n = t.shape[1] // CHUNK
        return t.reshape(B, n, CHUNK, GLA_HEADS, t.shape[-1]).transpose(1, 0, 3, 2, 4)

    qc, kc, vc, ac = prep(q), prep(k), prep(v), prep(log_a)
    S0 = jnp.zeros((B, GLA_HEADS, GLA_DK, GLA_DV), jnp.float32)
    _, o = lax.scan(gla_chunk_step, S0, (qc, kc, vc, ac))
    o = o.transpose(1, 0, 3, 2, 4).reshape(B, -1, GLA_HEADS, GLA_DV)[:, pad:]
    return o.astype(v.dtype)

def hybrid_mixer(u, w_in, w_pool_mix, pool_scale, w_pool_out, w_gate_up, b_gate, gla_norm, w_gla_out, w_out):
    B, L, _ = u.shape
    z = jnp.einsum('bld,dn->bln', u, w_in)
    a, q, k, v, r, lr, ga, gb = jnp.split(z, IN_SPLITS, axis=-1)
    p = multiscale_pool(a).reshape(B, L, POOL_GROUPS, POOL_GROUP_DIM)
    p = jnp.einsum('blgc,gce->blge', p, w_pool_mix).reshape(B, L, POOL_WIDTH) * pool_scale
    y_a = jnp.einsum('blc,cd->bld', p, w_pool_out)
    log_a = jax.nn.log_sigmoid((lr @ w_gate_up + b_gate).astype(jnp.float32)) / GLA_TAU
    q = q.reshape(B, L, GLA_HEADS, GLA_DK) * (GLA_DK ** -0.5)
    k = k.reshape(B, L, GLA_HEADS, GLA_DK)
    v = v.reshape(B, L, GLA_HEADS, GLA_DV)
    log_a = log_a.reshape(B, L, GLA_HEADS, GLA_DK)
    o = gla_chunked(q, k, v, log_a)
    o = rmsnorm(o, gla_norm.reshape(GLA_HEADS, GLA_DV)) * jax.nn.silu(r).reshape(B, L, GLA_HEADS, GLA_DV)
    y_b = jnp.einsum('blc,cd->bld', o.reshape(B, L, GLA_VAL), w_gla_out)
    m = jax.nn.sigmoid(ga) * y_a + jax.nn.sigmoid(gb) * y_b
    return jnp.einsum('bld,de->ble', m, w_out)

def squared_relu_mlp(u, w_ff1, w_ff2):
    hdn = jnp.square(jax.nn.relu(jnp.einsum('bld,df->blf', u, w_ff1)))
    return jnp.einsum('blf,fd->bld', hdn, w_ff2)

def first_inputs(seed: int = 0) -> dict:
    key = jax.random.key(seed)
    ks = jax.random.split(key, 20)
    f32 = jnp.float32
    nrm = lambda k, shape, s: jax.random.normal(k, shape, f32) * s
    return {
        "x": jax.random.normal(ks[0], (BATCH, SEQ, D_MODEL), f32),
        "meta_tokens": nrm(ks[1], (N_META, D_MODEL), 1.0),
        "norm_mix": 1.0 + nrm(ks[2], (DEPTH, D_MODEL), 0.05),
        "w_in": nrm(ks[3], (DEPTH, D_MODEL, N_IN), D_MODEL ** -0.5),
        "w_pool_mix": nrm(ks[4], (DEPTH, POOL_GROUPS, POOL_GROUP_DIM, POOL_GROUP_DIM), POOL_GROUP_DIM ** -0.5),
        "pool_scale": 1.0 + nrm(ks[5], (DEPTH, POOL_WIDTH), 0.1),
        "w_pool_out": nrm(ks[6], (DEPTH, POOL_WIDTH, D_MODEL), POOL_WIDTH ** -0.5),
        "w_gate_up": nrm(ks[7], (DEPTH, GLA_GATE_RANK, GLA_KEY), GLA_GATE_RANK ** -0.5),
        "b_gate": nrm(ks[8], (DEPTH, GLA_KEY), 0.1),
        "gla_norm": 1.0 + nrm(ks[9], (DEPTH, GLA_VAL), 0.05),
        "w_gla_out": nrm(ks[10], (DEPTH, GLA_VAL, D_MODEL), GLA_VAL ** -0.5),
        "w_out": nrm(ks[11], (DEPTH, D_MODEL, D_MODEL), D_MODEL ** -0.5),
        "norm_ffn": 1.0 + nrm(ks[12], (DEPTH, D_MODEL), 0.05),
        "w_ff1": nrm(ks[13], (DEPTH, D_MODEL, D_FF), D_MODEL ** -0.5),
        "w_ff2": nrm(ks[14], (DEPTH, D_FF, D_MODEL), D_FF ** -0.5),
        "norm_final": 1.0 + nrm(ks[15], (D_MODEL,), 0.05),
    }

def first_block(x, meta_tokens, norm_mix, w_in, w_pool_mix, pool_scale, w_pool_out, w_gate_up, b_gate,
              gla_norm, w_gla_out, w_out, norm_ffn, w_ff1, w_ff2, norm_final):
    B = x.shape[0]
    meta = jnp.broadcast_to(meta_tokens[None].astype(x.dtype), (B, N_META, D_MODEL))
    h = jnp.concatenate([meta, x], axis=1)
    for l in range(DEPTH):
        h = h + hybrid_mixer(rmsnorm(h, norm_mix[l]), w_in[l], w_pool_mix[l], pool_scale[l], w_pool_out[l],
                             w_gate_up[l], b_gate[l], gla_norm[l], w_gla_out[l], w_out[l])
        h = h + squared_relu_mlp(rmsnorm(h, norm_ffn[l]), w_ff1[l], w_ff2[l])
    return rmsnorm(h, norm_final)[:, N_META:]


MEM_LEN = 256
D_MIX = D_MODEL
D_RWKV = D_MIX // 2
D_CONV = D_MIX - D_RWKV
RWKV_HEAD = 64
RWKV_HEADS = D_RWKV // RWKV_HEAD
CONV_WIDTH = 31
DECAY_LORA = 64
AAA_LORA = 64
MV_LORA = 32
GATE_LORA = 128
XA_HEADS = 4
XA_HEAD_DIM = D_MODEL // XA_HEADS
D_FF_2 = -(-8 * D_MODEL // (3 * 256)) * 256
RMS_EPS = 1e-6
LN_EPS = 1e-5
GN_EPS = 64e-5
DECAY_SCALE = math.exp(-0.5)

N_RWKV_COLS = 3 * D_RWKV + DECAY_LORA + AAA_LORA + GATE_LORA
N_IN_FIRST = 2 * D_CONV + N_RWKV_COLS
N_IN_REST = N_IN_FIRST + MV_LORA


def rms_norm(x, g):
    xf = x.astype(jnp.float32)
    y = xf * lax.rsqrt(jnp.mean(xf * xf, axis=-1, keepdims=True) + RMS_EPS)
    return (y * g.astype(jnp.float32)).astype(x.dtype)

def layer_norm(x, g, b):
    xf = x.astype(jnp.float32)
    mean = jnp.mean(xf, axis=-1, keepdims=True)
    var = jnp.mean(jnp.square(xf - mean), axis=-1, keepdims=True)
    y = (xf - mean) * lax.rsqrt(var + LN_EPS)
    return (y * g.astype(jnp.float32) + b.astype(jnp.float32)).astype(x.dtype)

def token_shift_mix(p, mu):
    prev = jnp.pad(p, ((0, 0), (1, 0), (0, 0)))[:, :-1]
    return p + mu * (prev - p)

def conformer_conv(u, conv_w, conv_b, ln_g, ln_b):
    h = u[..., :D_CONV] * jax.nn.sigmoid(u[..., D_CONV:])
    h = lax.conv_general_dilated(
        h, conv_w[:, None, :], window_strides=(1,), padding=[(CONV_WIDTH - 1, 0)],
        dimension_numbers=("NWC", "WIO", "NWC"), feature_group_count=D_CONV) + conv_b
    h = layer_norm(h, ln_g, ln_b)
    return jax.nn.silu(h)

def rwkv7_recurrence(r, w, k, v, kk, a):
    B = r.shape[0]
    tm = lambda z: jnp.moveaxis(z.astype(jnp.float32), 1, 0)

    def step(S, inp):
        r_t, w_t, k_t, v_t, kk_t, a_t = inp
        s_kk = jnp.einsum("bhvk,bhk->bhv", S, kk_t)
        S = (S * w_t[:, :, None, :]
             - s_kk[..., None] * (kk_t * a_t)[:, :, None, :]
             + v_t[..., None] * k_t[:, :, None, :])
        return S, jnp.einsum("bhvk,bhk->bhv", S, r_t)

    S0 = jnp.zeros((B, RWKV_HEADS, RWKV_HEAD, RWKV_HEAD), jnp.float32)
    _, y = lax.scan(step, S0, (tm(r), tm(w), tm(k), tm(v), tm(kk), tm(a)))
    return jnp.moveaxis(y, 0, 1)

def rwkv7_mix(p, mu, w0, w_up, a0, a_up, g_up, k_k, k_a, r_k, lnx_g, lnx_b, v_first, v0, v_up):
    B, T = p.shape[:2]
    p = token_shift_mix(p, mu)
    o = 0
    r = p[..., o:o + D_RWKV]; o += D_RWKV
    k = p[..., o:o + D_RWKV]; o += D_RWKV
    v = p[..., o:o + D_RWKV]; o += D_RWKV
    w_lo = p[..., o:o + DECAY_LORA]; o += DECAY_LORA
    a_lo = p[..., o:o + AAA_LORA]; o += AAA_LORA
    g_lo = p[..., o:o + GATE_LORA]; o += GATE_LORA

    log_w = -DECAY_SCALE * jax.nn.sigmoid((w0 + jnp.tanh(w_lo) @ w_up).astype(jnp.float32))
    w = jnp.exp(log_w)
    a = jax.nn.sigmoid(a0 + a_lo @ a_up)
    g = jax.nn.sigmoid(g_lo) @ g_up
    if v_first is None:
        v_first = v
    else:
        vres_lo = p[..., o:o + MV_LORA]
        v = v + (v_first - v) * jax.nn.sigmoid(v0 + vres_lo @ v_up)

    hd = lambda z: z.reshape(B, T, RWKV_HEADS, RWKV_HEAD)
    kk = hd(k * k_k).astype(jnp.float32)
    kk = kk * lax.rsqrt(jnp.maximum(jnp.sum(kk * kk, axis=-1, keepdims=True), 1e-24))
    k = k * (1.0 + (a - 1.0) * k_a)
    rh, kh, vh = hd(r), hd(k), hd(v)

    y = rwkv7_recurrence(rh, hd(w), kh, vh, kk, hd(a))
    mean = jnp.mean(y, axis=-1, keepdims=True)
    var = jnp.mean(jnp.square(y - mean), axis=-1, keepdims=True)
    y = (y - mean) * lax.rsqrt(var + GN_EPS)
    gn_g = lnx_g.reshape(RWKV_HEADS, RWKV_HEAD).astype(jnp.float32)
    gn_b = lnx_b.reshape(RWKV_HEADS, RWKV_HEAD).astype(jnp.float32)
    y = y * gn_g + gn_b
    bonus = jnp.sum((rh * kh * r_k).astype(jnp.float32), axis=-1, keepdims=True) * vh.astype(jnp.float32)
    y = (y + bonus).astype(p.dtype).reshape(B, T, D_RWKV) * g
    return y, v_first

def memory_cross_attention(h, mem_n, wq, wkv, wo):
    B, T, _ = h.shape
    M = mem_n.shape[1]
    q = (h @ wq).reshape(B, T, XA_HEADS, XA_HEAD_DIM)
    kv = mem_n @ wkv
    km = kv[..., :D_MODEL].reshape(B, M, XA_HEADS, XA_HEAD_DIM)
    vm = kv[..., D_MODEL:].reshape(B, M, XA_HEADS, XA_HEAD_DIM)
    s = jnp.einsum("bthd,bmhd->bhtm", q, km).astype(jnp.float32) * (XA_HEAD_DIM ** -0.5)
    pr = jax.nn.softmax(s, axis=-1).astype(vm.dtype)
    o = jnp.einsum("bhtm,bmhd->bthd", pr, vm).reshape(B, T, D_MODEL)
    return o @ wo

def swiglu(h, w_gu, w_down):
    gu = h @ w_gu
    return (jax.nn.silu(gu[..., :D_FF_2]) * gu[..., D_FF_2:]) @ w_down

def second_inputs(seed: int = 0) -> dict:
    key = jax.random.key(seed)
    ks = iter(jax.random.split(key, 40))
    nrm = lambda shape, s: jax.random.normal(next(ks), shape, jnp.float32) * s
    uni = lambda shape: jax.random.uniform(next(ks), shape, jnp.float32)
    L, Lr = DEPTH, DEPTH - 1
    return {
        "x": nrm((BATCH, SEQ, D_MODEL), 1.0),
        "mem": nrm((BATCH, MEM_LEN, D_MODEL), 1.0),
        "mem_norm_g": 1.0 + nrm((D_MODEL,), 0.05),
        "norm_gains": 1.0 + nrm((L, 6, D_MODEL), 0.05),
        "w_in_first": nrm((D_MODEL, N_IN_FIRST), D_MODEL ** -0.5),
        "w_in_rest": nrm((Lr, D_MODEL, N_IN_REST), D_MODEL ** -0.5),
        "mu_first": uni((N_RWKV_COLS,)),
        "mu_rest": uni((Lr, N_RWKV_COLS + MV_LORA)),
        "conv_w": nrm((L, CONV_WIDTH, D_CONV), CONV_WIDTH ** -0.5),
        "conv_b": nrm((L, D_CONV), 0.02),
        "conv_ln_g": 1.0 + nrm((L, D_CONV), 0.05),
        "conv_ln_b": nrm((L, D_CONV), 0.02),
        "w0": nrm((L, D_RWKV), 1.0),
        "w_up": nrm((L, DECAY_LORA, D_RWKV), DECAY_LORA ** -0.5),
        "a0": nrm((L, D_RWKV), 0.1),
        "a_up": nrm((L, AAA_LORA, D_RWKV), AAA_LORA ** -0.5),
        "g_up": nrm((L, GATE_LORA, D_RWKV), GATE_LORA ** -0.5),
        "v0": nrm((Lr, D_RWKV), 0.1),
        "v_up": nrm((Lr, MV_LORA, D_RWKV), MV_LORA ** -0.5),
        "k_k": 0.85 + nrm((L, D_RWKV), 0.05),
        "k_a": 1.0 + nrm((L, D_RWKV), 0.05),
        "r_k": nrm((L, RWKV_HEADS, RWKV_HEAD), 0.1),
        "lnx_g": 1.0 + nrm((L, D_RWKV), 0.05),
        "lnx_b": nrm((L, D_RWKV), 0.02),
        "w_out": nrm((L, D_MIX, D_MODEL), D_MIX ** -0.5),
        "wq": nrm((L, D_MODEL, D_MODEL), D_MODEL ** -0.5),
        "wkv": nrm((L, D_MODEL, 2 * D_MODEL), D_MODEL ** -0.5),
        "wo": nrm((L, D_MODEL, D_MODEL), D_MODEL ** -0.5),
        "w_gu": nrm((L, D_MODEL, 2 * D_FF_2), D_MODEL ** -0.5),
        "w_down": nrm((L, D_FF_2, D_MODEL), D_FF_2 ** -0.5),
    }

def second_block(x, mem, mem_norm_g, norm_gains, w_in_first, w_in_rest, mu_first, mu_rest,
              conv_w, conv_b, conv_ln_g, conv_ln_b, w0, w_up, a0, a_up, g_up, v0, v_up,
              k_k, k_a, r_k, lnx_g, lnx_b, w_out, wq, wkv, wo, w_gu, w_down):
    mem_n = rms_norm(mem, mem_norm_g)
    v_first = None
    for i in range(DEPTH):
        g = norm_gains[i]
        h = rms_norm(x, g[0])
        if i == 0:
            p = h @ w_in_first
            mu, vr0, vr_up = mu_first, None, None
        else:
            p = h @ w_in_rest[i - 1]
            mu, vr0, vr_up = mu_rest[i - 1], v0[i - 1], v_up[i - 1]
        y_conv = conformer_conv(p[..., :2 * D_CONV], conv_w[i], conv_b[i], conv_ln_g[i], conv_ln_b[i])
        y_rwkv, v_first = rwkv7_mix(p[..., 2 * D_CONV:], mu, w0[i], w_up[i], a0[i], a_up[i], g_up[i],
                                    k_k[i], k_a[i], r_k[i], lnx_g[i], lnx_b[i], v_first, vr0, vr_up)
        y = jnp.concatenate([y_conv, y_rwkv], axis=-1) @ w_out[i]
        x = x + rms_norm(y, g[1])
        y = memory_cross_attention(rms_norm(x, g[2]), mem_n, wq[i], wkv[i], wo[i])
        x = x + rms_norm(y, g[3])
        y = swiglu(rms_norm(x, g[4]), w_gu[i], w_down[i])
        x = x + rms_norm(y, g[5])
    return x


def setup_inputs(seed=0):
    out = dict(first_inputs(seed))
    for name, value in second_inputs(seed + 1).items():
        if name != "x":
            out[name + "_2"] = value
    return out


def reference(
    x, meta_tokens, norm_mix, w_in, w_pool_mix, pool_scale, w_pool_out, w_gate_up, b_gate,
    gla_norm, w_gla_out, w_out, norm_ffn, w_ff1, w_ff2, norm_final, mem_2, mem_norm_g_2,
    norm_gains_2, w_in_first_2, w_in_rest_2, mu_first_2, mu_rest_2, conv_w_2, conv_b_2,
    conv_ln_g_2, conv_ln_b_2, w0_2, w_up_2, a0_2, a_up_2, g_up_2, v0_2, v_up_2, k_k_2, k_a_2,
    r_k_2, lnx_g_2, lnx_b_2, w_out_2, wq_2, wkv_2, wo_2, w_gu_2, w_down_2,
):
    x = first_block(
        x, meta_tokens, norm_mix, w_in, w_pool_mix, pool_scale, w_pool_out, w_gate_up, b_gate,
        gla_norm, w_gla_out, w_out, norm_ffn, w_ff1, w_ff2, norm_final,
    )
    return second_block(
        x, mem_2, mem_norm_g_2, norm_gains_2, w_in_first_2, w_in_rest_2, mu_first_2, mu_rest_2,
        conv_w_2, conv_b_2, conv_ln_g_2, conv_ln_b_2, w0_2, w_up_2, a0_2, a_up_2, g_up_2, v0_2,
        v_up_2, k_k_2, k_a_2, r_k_2, lnx_g_2, lnx_b_2, w_out_2, wq_2, wkv_2, wo_2, w_gu_2,
        w_down_2,
    )


_drawn_inputs = setup_inputs


def setup_inputs(seed=0):
    import zlib

    import numpy as np

    out = dict(_drawn_inputs(seed))
    spreads = {}
    factors = {'b_gate': 3.307, 'gla_norm': 2.672, 'conv_ln_b_2': 4.667, 'k_k_2': 5.777, 'lnx_b_2': 5.768}
    for name, (base, spread) in spreads.items():
        noise = np.random.default_rng([zlib.crc32(name.encode()), seed]).standard_normal(out[name].shape)
        drawn = base * np.exp(spread * noise) if base else spread * noise
        out[name] = __import__('jax').numpy.asarray(drawn.astype(out[name].dtype))
    for name, factor in factors.items():
        out[name] = (out[name] * factor).astype(out[name].dtype)
    return out
```

```python
import concourse.bass as bass
from concourse import mybir
from contextlib import ExitStack
import math

P = 128
UNIT = 2048
DECAY = math.exp(-0.5)

VECS = [("norm_mix", 8), ("pool_scale", 4), ("b_gate", 2), ("gla_norm", 4), ("norm_ffn", 8), ("norm_final", 8),
        ("mem_norm_g_2", 8), ("norm_gains_2", 48), ("mu_first_2", 14), ("conv_w_2", 124), ("conv_b_2", 4),
        ("conv_ln_g_2", 4), ("conv_ln_b_2", 4), ("w0_2", 4), ("a0_2", 4), ("k_k_2", 4), ("k_a_2", 4),
        ("r_k_2", 4), ("lnx_g_2", 4), ("lnx_b_2", 4)]
NV = sum(n for _, n in VECS)
EPSCOLS = [1e-6, 1e-5, 64e-5, 0.0]
MATS = ["ones1024", "ones512", "ones128", "blk", "blk64", "ident"]
NCF = len(MATS) * 128 + len(EPSCOLS)
MASKS = [f"g{i}" for i in range(7)] + ["le", "lt"] + [f"u{i}" for i in range(6)] + [f"l{i}" for i in range(6)]
NCU = len(MASKS) * 128 + 2 * 128 + 528 + 512


def vcol(name):
    c = 0
    for n, k in VECS:
        if n == name:
            return c
        c += k
    raise KeyError(name)


def unit_list():
    u = []

    def t(tag, w, r0, nk, cols, width=128, kind="T"):
        u.append((tag, w, r0, nk, tuple(cols), width, kind))

    def pair(tag, w, c0, n, nk=8, r0=0):
        for i in range(n):
            t(tag, w, r0, nk, (c0 + 256 * i, c0 + 256 * i + 128))

    pair("a", "w_in", 0, 2)
    pair("k", "w_in", 768, 1)
    t("lr", "w_in", 0, 8, (2048,), 16)
    pair("q", "w_in", 512, 1)
    for i in range(2):
        t("v", "w_in", 0, 8, (1024 + 256 * i,), 256, "M")
    for i in range(2):
        t("po", "w_pool_out", 0, 4, [512 * i + 128 * j for j in range(4)])
    pair("r", "w_in", 1536, 2)
    pair("ga", "w_in", 2064, 4)
    pair("gb", "w_in", 3088, 4)
    for i in range(2):
        t("go", "w_gla_out", 0, 4, [512 * i + 128 * j for j in range(4)])
    pair("wo", "w_out", 0, 4)
    for g in range(4):
        pair("f1", "w_ff1", 1024 * g, 4)
        pair("f2", "w_ff2", 0, 4, 8, 1024 * g)
    pair("p", "w_in_first_2", 1024 + 1536, 1)
    for i in range(4):
        t("p", "w_in_first_2", 0, 8, (1024 + 512 + 128 * i, 1024 + 128 * i))
        if i % 2:
            t("p", "w_in_first_2", 0, 8, (2048 + 128 * (i - 1), 2048 + 128 * i))
    for i in range(4):
        t("cv", "w_in_first_2", 0, 8, (128 * i, 512 + 128 * i))
    pair("wo2", "w_out_2", 0, 4)
    pair("km", "wkv_2", 0, 4)
    for i in range(4):
        t("vm", "wkv_2", 0, 8, (1024 + 256 * i,), 256, "M")
    pair("wq", "wq_2", 0, 4)
    pair("xo", "wo_2", 0, 4)
    for g in range(3):
        nt = 8 if g < 2 else 6
        for i in range(nt):
            t("gu", "w_gu_2", 0, 8, (1024 * g + 128 * i, 2816 + 1024 * g + 128 * i))
        pair("dn", "w_down_2", 0, 4, nt, 1024 * g)
    return u


def unit_size(u):
    return u[3] * len(u[4]) * u[5]


class Tok:

    def __init__(self, eng):
        self.eng, self.used, self.sem, self.val = eng, False, None, 0


class Bank:
    def __init__(self, ap):
        self.ap, self.free = ap, []


def program(nc, wstream, vecs, cf, cu, xT, metaT, memT, pmix, gup, wau, gupg, out, dumps=None):
    f32, f32r, u8 = mybir.dt.float32, mybir.dt.float32r, mybir.dt.uint8
    ALU, ACT = mybir.AluOpType, mybir.ActivationFunctionType
    ctx = ExitStack()
    with ctx:
        def sb(name, shape, dt=f32):
            return ctx.enter_context(nc.sbuf_tensor(name, shape, dt))

        raw = [sb(f"raw{i}", [P, UNIT]) for i in range(2)]
        WH = [sb(f"wh{i}", [P, UNIT], f32r) for i in range(2)]
        WL = [sb(f"wl{i}", [P, UNIT], f32r) for i in range(2)]
        V = sb("vecs_sb", [P, NV + 8])
        C = sb("cf_sb", [P, NCF])
        U = sb("cu_sb", [P, NCU], u8)
        mh = sb("mh", [P, 8, 16])
        muh = sb("muh", [P, 8, 16], f32r)
        mul_ = sb("mul", [P, 8, 16], f32r)
        msq = sb("msq", [P, 2, 16])
        mrs = sb("mrs", [P, 16])
        rcol = sb("rcol", [P, 8])
        lrs = sb("lrs", [16, 528])
        gup_sb = sb("gup_sb", [16, 256])
        khm = sb("khm", [16, 256])
        vmeta = sb("vmeta", [16, 512])
        sm = sb("sm", [P, 64])
        cuts = [0, 8, 24, 34, 47, 55, 70]

        class Zone:

            def __init__(self, tag, dt):
                self.parts = []
                for a, b_ in zip(cuts, cuts[1:]):
                    pad = nc.sbuf_tensor(f"pad_{tag}{a}", [P, 512 * a], f32) if a else None
                    if pad:
                        pad.__enter__()
                    g = nc.sbuf_tensor(f"{tag}{a}", [P, 512 * (b_ - a)], dt)
                    self.parts.append((a * 512, b_ * 512, g.__enter__()))
                    g.__exit__(None, None, None)
                    if pad:
                        pad.__exit__(None, None, None)

            def __getitem__(self, key):
                a, b_ = key[1].start, key[1].stop
                for p0, p1, t in self.parts:
                    if p0 <= a and b_ <= p1:
                        return t[:, a - p0:b_ - p0]
                raise ValueError((a, b_))

        ZF, ZR = Zone("zf", f32), Zone("zr", f32r)
        sb("zone", [P, 512 * cuts[-1]])
        banks = [Bank(ctx.enter_context(nc.psum_tensor(f"ps{i}", [P, 512], f32))) for i in range(8)]

        def F(s, n=512):
            return ZF[:, s * 512:s * 512 + n]

        def R(s, n=512):
            return ZR[:, s * 512:s * 512 + n]

        def vec(name, i=0):
            c = vcol(name) + i
            return V[:, c:c + 1]

        def mat(name):
            i = MATS.index(name)
            return C[:, i * 128:(i + 1) * 128]

        def eps(i):
            return C[:, len(MATS) * 128 + i:len(MATS) * 128 + i + 1]

        def mask(name):
            i = MASKS.index(name)
            return U[:, i * 128:(i + 1) * 128]

        def mask4(name):
            return mask(name).unsqueeze(1).to_broadcast([P, 4, 128])

        RS528 = U[:, len(MASKS) * 128 + 256:len(MASKS) * 128 + 256 + 528]
        RS512 = U[:, len(MASKS) * 128 + 256 + 528:NCU]

        names = ["pe", "act", "dve", "pool", "sp"]
        Q = {n: [] for n in names}
        esem = {n: ctx.enter_context(nc.semaphore(f"s_{n}")) for n in names[:4]}
        dsem, dcount = {}, {}

        def flat(x):
            for y in x:
                if y is None:
                    continue
                if isinstance(y, (list, tuple)):
                    yield from flat(y)
                else:
                    yield y

        def op(eng, fn, *after):
            after = list(flat(after))
            for t in after:
                t.used = True
            tok = Tok(eng)
            Q[eng].append((after, fn, tok))
            return tok

        def pe(fn, *a):
            return op("pe", fn, *a)

        def act(fn, *a):
            return op("act", fn, *a)

        def dve(fn, *a):
            return op("dve", fn, *a)

        def pool(fn, *a):
            return op("pool", fn, *a)

        def dma(sem, dst, src, *after):
            if sem not in dsem:
                dsem[sem] = ctx.enter_context(nc.semaphore(f"d_{sem}"))
                dcount[sem] = 0
            dcount[sem] += 16
            tok = op("sp", lambda e: e.dma_start(dst, src), *after)
            tok.eng, tok.sem, tok.val = "dma", dsem[sem], dcount[sem]
            return tok

        def A(out_, in_, fn, *after, scale=1.0, bias=0.0):
            return act(lambda e: e.activation(out_, in_, fn, bias=bias, scale=scale), *after)

        def copyA(out_, in_, *after, scale=1.0):
            return act(lambda e: e.activation(out_, in_, ACT.Copy, scale=scale), *after)

        def TT(out_, a, b, o, *after, eng="dve"):
            return op(eng, lambda e: e.tensor_tensor(out_, a, b, o), *after)

        def TS(out_, a, s1, o1, *after, s2=None, o2=None, eng="dve"):
            if o2 is None:
                return op(eng, lambda e: e.tensor_scalar(out_, a, s1, None, o1), *after)
            return op(eng, lambda e: e.tensor_scalar(out_, a, s1, s2, o1, o2), *after)

        def STT(out_, a, s, b, o1, o2, *after):
            return dve(lambda e: e.scalar_tensor_tensor(out=out_, in0=a, scalar=s, in1=b, op0=o1, op1=o2), *after)

        def RCP(out_, a, *after):
            return dve(lambda e: e.reciprocal(out_, a), *after)

        def MM(out_, l, r, *after, start=True, stop=True):
            return pe(lambda e: e.matmul(out_, l, r, start=start, stop=stop), *after)

        def TR(out_, in_, idn, *after):
            return pe(lambda e: e.transpose(out_, in_, idn), *after)

        def rb(ap):
            return ap.bitcast(f32)

        def split(hi, lo, src, *after, eng="dve"):
            a = copyA(hi, src, *after)
            return [a, TT(lo, src, rb(hi), ALU.subtract, a, eng=eng)]

        def split_scaled(hi, lo, src, s, *after):
            a = copyA(hi, src, *after, scale=s)
            return [a, STT(lo, src, s, rb(hi), ALU.mult, ALU.subtract, a)]

        DB, MB = banks[:3], banks[3:]

        def acq(pool_):
            return pool_.pop(0)

        def rel(pool_, b, *toks):
            b.free = list(flat(toks))
            pool_.append(b)

        units = unit_list()
        offs, o = [], 0
        for u in units:
            offs.append(o)
            o += unit_size(u) * P
        wd, ws, wdone = {}, {}, {}
        nxt = [0]

        def wdma(n):
            if n >= len(units) or n in wd:
                return
            sz = unit_size(units[n])
            src = wstream[offs[n]:offs[n] + P * sz].rearrange("(p n) -> p n", n=sz)
            wd[n] = dma(f"w{n % 2}", raw[n % 2][:, 0:sz], src, ws.get(n - 2))

        def wsplit(n):
            if n >= len(units) or n in ws:
                return
            sz = unit_size(units[n])
            cuts = [(0, sz)] if sz <= 1024 else [(0, 1024), (1024, sz)]
            toks = []
            for a, b in cuts:
                h, l, r_ = WH[n % 2][:, a:b], WL[n % 2][:, a:b], raw[n % 2][:, a:b]
                t = copyA(h, r_, wd[n], wdone.get(n - 2))
                toks.append([t, TT(l, r_, rb(h), ALU.subtract, t, wdone.get(n - 2))])
            ws[n] = toks

        def wunit(tag):
            n = nxt[0]
            nxt[0] += 1
            assert units[n][0] == tag, (units[n], tag)
            wdma(n)
            wdma(n + 1)
            wsplit(n)
            wsplit(n + 1)
            wdma(n + 2)
            return n, units[n], WH[n % 2], WL[n % 2]

        bgs = []

        def step_bg():
            for g_ in list(bgs):
                try:
                    next(g_)
                except StopIteration:
                    bgs.remove(g_)

        def drain_bg(*gs):
            for g_ in gs or list(bgs):
                while g_ in bgs:
                    try:
                        next(g_)
                    except StopIteration:
                        bgs.remove(g_)

        def tile_T(unit, j, xs, N, evac, meta=None):
            n, u, wh, wl = unit
            nk, w = u[3], u[5]
            b = acq(DB)
            mb = acq(DB) if meta else None
            last = None
            for k in range(nk):
                c = (j * nk + k) * w
                lh, ll = wh[:, c:c + w], wl[:, c:c + w]
                xh, xl, xt = xs[k]
                wt = ws[n][min(c // 1024, len(ws[n]) - 1)]

                def go(e, lh=lh, ll=ll, xh=xh, xl=xl, k=k):
                    e.matmul(b.ap[0:w, 0:N], lh, xh, start=(k == 0), stop=False)
                    e.matmul(b.ap[0:w, 0:N], lh, xl, start=False, stop=False)
                    return e.matmul(b.ap[0:w, 0:N], ll, xh, start=False, stop=(k == nk - 1))
                last = pe(go, wt, xt, b.free if k == 0 else None)
            if meta:
                for k in range(nk):
                    c = (j * nk + k) * w
                    lh, ll = wh[:, c:c + w], wl[:, c:c + w]
                    xh, xl, xt = meta[k]

                    def go(e, lh=lh, ll=ll, xh=xh, xl=xl, k=k):
                        e.matmul(mb.ap[0:w, 0:16], lh, xh, start=(k == 0), stop=False)
                        e.matmul(mb.ap[0:w, 0:16], lh, xl, start=False, stop=False)
                        return e.matmul(mb.ap[0:w, 0:16], ll, xh, start=False, stop=(k == nk - 1))
                    last = pe(go, xt, mb.free if k == 0 else None)
            wdone[n] = last
            if meta:
                t, tm = evac(b.ap[0:w, 0:N], mb.ap[0:w, 0:16], last)
                rel(DB, b, t)
                rel(DB, mb, tm)
            else:
                rel(DB, b, evac(b.ap[0:w, 0:N], last))
            step_bg()
            return last

        def tile_M(unit, xs, t0, tn, evac):
            n, u, wh, wl = unit
            nk = u[3]
            b = acq(DB)
            for k in range(nk):
                rh, rl = wh[:, k * 256:k * 256 + 256], wl[:, k * 256:k * 256 + 256]
                xh, xl, xt = xs[k]
                xh, xl = xh[:, t0:t0 + tn], xl[:, t0:t0 + tn]
                wt = ws[n][min(k * 256 // 1024, len(ws[n]) - 1)]

                def go(e, rh=rh, rl=rl, xh=xh, xl=xl, k=k):
                    e.matmul(b.ap[0:tn, 0:256], xh, rh, start=(k == 0), stop=False)
                    e.matmul(b.ap[0:tn, 0:256], xh, rl, start=False, stop=False)
                    return e.matmul(b.ap[0:tn, 0:256], xl, rh, start=False, stop=(k == nk - 1))
                last = pe(go, wt, xt, b.free if k == 0 else None)
            wdone[n] = last
            rel(DB, b, evac(b.ap[0:tn, 0:256], last))
            step_bg()

        class Stat:

            def __init__(self, acc, tmps, N=512, free=None):
                self.acc, self.tmps, self.N, self.n, self.t = acc, tmps, N, 0, free
                self.tt = [free] * len(tmps)

            def add(self, src, *after, scale=1.0):
                if self.n == 0:
                    self.t = A(self.acc, src, ACT.Square, self.t, *after, scale=scale)
                    r_ = self.t
                else:
                    i = self.n % len(self.tmps)
                    tmp = self.tmps[i]
                    r_ = A(tmp, src, ACT.Square, self.tt[i], *after, scale=scale)
                    self.t = TT(self.acc, self.acc, tmp, ALU.add, r_, self.t, eng="pool")
                    self.tt[i] = self.t
                self.n += 1
                return r_

            def mean(self, m="ones1024", pool_=DB):
                b = acq(pool_)
                return b, MM(b.ap[:, 0:self.N], mat(m), self.acc, self.t, b.free, TCF)

            def rstd(self, dst, e_=0, m="ones1024", pool_=DB, free=None):
                b, t = self.mean(m, pool_)
                s = A(dst, b.ap[:, 0:self.N], ACT.Sqrt, t, free, bias=eps(e_))
                rel(pool_, b, s)
                self.done = t
                return RCP(dst, dst, s)

        TV = dma("v", V[:, 0:NV], vecs)
        hx = []
        xv = xT.rearrange("(k p) t -> p k t", p=P)
        wdma(0)
        TCF = dma("cf", C[:, :], cf)
        tm_ = dma("mh", mh[:, :, :], metaT.rearrange("(k p) t -> p k t", p=P))
        for k in range(8):
            hx.append(dma(f"x{k}", F(k), xv[:, k, :]))
        wdma(1)
        cu_raw = F(55, NCU)
        TCU = dma("cu", cu_raw, cu)
        TCU = dve(lambda e: e.tensor_copy(U[:, :], cu_raw), TCU)
        pmx = F(54)
        tpm = dma("pm", pmx, pmix)
        tgu = dma("gu", gup_sb[:, :], gup)

        ACC, TMP, RSTD, TMP2 = F(66), F(67), F(68), F(69)

        st = Stat(ACC, [TMP, TMP2])
        stm = Stat(msq[:, 0, :], [msq[:, 1, :]], 16)
        xs, ms = [], []
        for k in range(8):
            t = split_scaled(R(8 + k), R(16 + k), F(k), vec("norm_mix", k), hx[k], TV)
            xs.append((R(8 + k), R(16 + k), t))
            t = split_scaled(muh[:, k, :], mul_[:, k, :], mh[:, k, :], vec("norm_mix", k), tm_, TV)
            ms.append((muh[:, k, :], mul_[:, k, :], t))
        for k in range(8):
            st.add(F(k), hx[k])
            stm.add(mh[:, k, :], tm_)
        trs = st.rstd(RSTD)
        trm = stm.rstd(mrs[:, :])
        b = acq(DB)
        for i in range(4):
            t = MM(b.ap[:, i:i + 1], F(66)[:, i * 128:(i + 1) * 128], mat("ones1024")[:, 0:1], b.free)
        t = MM(b.ap[0:16, 4:5], msq[:, 0, :], mat("ones1024")[:, 0:1], b.free)
        t1 = A(rcol[:, 0:4], b.ap[:, 0:4], ACT.Sqrt, t, bias=eps(0))
        t2 = A(rcol[0:16, 4:5], b.ap[0:16, 4:5], ACT.Sqrt, t1, bias=eps(0)[0:16, :])
        rel(DB, b, t2)
        trc = [RCP(rcol[:, 0:4], rcol[:, 0:4], t1), RCP(rcol[0:16, 4:5], rcol[0:16, 4:5], t2)]

        def a_ap(i):
            return F(34, 2112)[:, i * 528:(i + 1) * 528]

        ta = [None] * 4
        for uu in range(2):
            un = wunit("a")
            for j in range(2):
                i = 2 * uu + j

                def ev(p, pm, t, i=i):
                    x = TT(a_ap(i)[:, 16:528], p, RSTD, ALU.mult, t, trs)
                    y = TT(a_ap(i)[:, 0:16], pm, mrs[:, :], ALU.mult, t, trm)
                    ta[i] = [x, y]
                    return x, y
                tile_T(un, j, xs, 512, ev, ms)

        pooled = [None] * 4

        def bg_pool():
            for gi in range(4):
                src, tk = a_ap(gi), ta[gi]
                cur, width = src, 1
                for s in range(gi + 1):
                    n0 = 2 * width - 1
                    dst = F(47, 528) if s % 2 == 0 else ZF[:, 47 * 512 + 528:47 * 512 + 1056]
                    tk = TT(dst[:, n0:528], cur[:, n0:528], cur[:, n0 - width:528 - width], ALU.add, tk,
                            pooled[gi - 1] if gi and s == 0 else None)
                    cur, width = dst, 2 * width
                pooled[gi] = STT(F(43 + gi), cur[:, 16:528], 1.0 / width, src[:, 16:528], ALU.mult, ALU.subtract, tk)
                yield

        bgp = bg_pool()
        bgs.append(bgp)

        def k_ap(i):
            return F(24, 1056)[:, i * 528:(i + 1) * 528]

        tk_ = [None] * 2
        un = wunit("k")
        for j in range(2):
            def ev(p, pm, t, i=j):
                x = TT(k_ap(i)[:, 16:528], p, RSTD, ALU.mult, t, trs)
                y = TT(k_ap(i)[:, 0:16], pm, mrs[:, :], ALU.mult, t, trm)
                tk_[i] = [x, y]
                return x, y
            tile_T(un, j, xs, 512, ev, ms)
        un = wunit("lr")
        tlr = []

        def ev(p, pm, t):
            x = TT(lrs[:, 16:528], p, RSTD[0:16, :], ALU.mult, t, trs)
            y = TT(lrs[:, 0:16], pm, mrs[0:16, :], ALU.mult, t, trm)
            tlr.extend([x, y])
            return x, y
        tile_T(un, 0, xs, 512, ev, ms)
        un = wunit("q")
        tq = [None] * 2
        for j in range(2):
            def ev(p, t, i=j):
                tq[i] = STT(F(27 + i), p, 0.125, RSTD, ALU.mult, ALU.mult, t, trs)
                return tq[i]
            tile_T(un, j, xs, 512, ev)
        tv = [[] for _ in range(5)]
        for uu in range(2):
            un = wunit("v")
            for i in range(4):
                def ev(p, t, i=i, uu=uu):
                    x = TS(F(29 + i)[:, 256 * uu:256 * uu + 256], p, rcol[:, i:i + 1], ALU.mult, t, trc)
                    tv[i].append(x)
                    return x
                tile_M(un, xs, 128 * i, 128, ev)

            def ev(p, t, uu=uu):
                x = TS(vmeta[:, 256 * uu:256 * uu + 256], p, rcol[0:16, 4:5], ALU.mult, t, trc)
                tv[4].append(x)
                return x
            tile_M(un, ms, 0, 16, ev)

        drain_bg(bgp)
        mixed = []
        for gi in range(4):
            b = acq(DB)
            t = MM(b.ap[:, :], pmx[:, gi * 128:(gi + 1) * 128], F(43 + gi), pooled, tpm, b.free)
            t1 = split_scaled(R(34 + gi), R(39 + gi), b.ap[:, :], vec("pool_scale", gi), t, ta, pooled)
            rel(DB, b, t1)
            mixed.append((R(34 + gi), R(39 + gi), t1))
            tmix = t

        state = {}

        def b_ap(i):
            return F(51, 1056)[:, i * 528:(i + 1) * 528]

        def bg_gla():
            tb = []
            Dm = [F(55 + i) for i in range(2)]
            for i in range(2):
                b = acq(MB)
                t = MM(b.ap[:, :], gup_sb[:, i * 128:(i + 1) * 128], lrs[:, 16:528], tlr, tgu, b.free)
                x, y = F(57), F(58)
                ts = []
                for (bk, n0, n1) in ((b, 16, 528), (None, 0, 16)):
                    if bk is None:
                        bk = acq(MB)
                        t = MM(bk.ap[:, 0:16], gup_sb[:, i * 128:(i + 1) * 128], lrs[:, 0:16], bk.free)
                    w = n1 - n0
                    prev = tb[-1] if tb else None
                    xx, yy = x[:, 0:w], y[:, 0:w]
                    if w == 16:
                        xx, yy = sm[:, 0:16], sm[:, 16:32]
                    a1 = A(xx, bk.ap[:, 0:w], ACT.Abs, t, prev, TCU, bias=vec("b_gate", i))
                    a2 = A(xx, xx, ACT.Exp, a1, scale=-1.0)
                    a3 = A(xx, xx, ACT.Ln, a2, bias=1.0)
                    m1 = TS(yy, bk.ap[:, 0:w], vec("b_gate", i), ALU.add, a1, prev, s2=0.0, o2=ALU.min)
                    rel(MB, bk, m1, a1)
                    ts.append(TT(b_ap(i)[:, n0:n1], yy, xx, ALU.subtract, a3, m1))
                    yield
                tb.append(dve(lambda e, i=i: e.tensor_tensor_scan(
                    ZF[:, 59 * 512 + i * 528:59 * 512 + (i + 1) * 528], RS528, b_ap(i), 0.0, ALU.mult, ALU.add), ts, TCU))
                yield

            def bs(i, n0=0, n1=528):
                return ZF[:, 59 * 512 + i * 528 + n0:59 * 512 + i * 528 + n1]
            tsc = [dve(lambda e, i=i: e.memset(F(62 + i), 0.0), TCU) for i in range(4)]
            prevm = None
            for l in range(7):
                if l < 6:
                    m = 32 >> l
                    fk = []
                    for i in range(2):
                        v3 = bs(i, 16, 528).rearrange("p (a b) -> p a b", b=2 * m)
                        ref = v3[:, :, m - 1:m].to_broadcast([P, 256 // m, 2 * m])
                        d3 = Dm[i].rearrange("p (a b) -> p a b", b=2 * m)
                        t = TT(d3, v3, ref, ALU.subtract, tb, state.get(("f", i)))
                        t = A(Dm[i], Dm[i], ACT.Abs, t)
                        t = A(Dm[i], Dm[i], ACT.Exp, t, scale=-1.0 / 16)
                        t1 = TT(F(57 + i), Dm[i], k_ap(i)[:, 16:528], ALU.mult, t, tk_[i], prevm, tb, eng="pool")
                        t2 = TT(F(51 + i), Dm[i], F(27 + i), ALU.mult, t, tq[i], prevm, tb, eng="pool")
                        state[("f", i)] = [t1, t2]
                        fk += [t1, t2]
                        yield
                    kk = [F(57 + i) for i in range(2)]
                    qq = [F(51 + i) for i in range(2)]
                else:
                    kk = [k_ap(i)[:, 16:528] for i in range(2)]
                    qq = [F(27 + i) for i in range(2)]
                    fk = []
                for tp_ in range(2):
                    bb_ = [acq(MB), acq(MB)]
                    for par in range(2):
                        lo = 64 * par
                        for tl_ in range(2):
                            cs = slice((2 * tp_ + tl_) * 128, (2 * tp_ + tl_ + 1) * 128)
                            for i in range(2):
                                t = MM(bb_[par].ap[:, (2 * tl_ + i) * 128:(2 * tl_ + i + 1) * 128], kk[i][lo:lo + 64, cs],
                                       qq[i][lo:lo + 64, cs], fk, bb_[par].free, tk_, tq)
                        z = 2 * tp_ + par
                        sc3 = F(62 + z).rearrange("p (a b) -> p a b", b=128)
                        ps3 = bb_[par].ap[:, :].rearrange("p (a b) -> p a b", b=128)
                        tsc[z] = dve(lambda e, sc3=sc3, ps3=ps3, l=l: e.copy_predicated(sc3, mask4(f"g{l}"), ps3),
                                     t, tsc[z], TCU)
                        rel(MB, bb_[par], tsc[z])
                        prevm = t
                    yield
            tqh, tkh = [], []
            for i in range(2):
                t = A(Dm[i], bs(i, 16, 528), ACT.Exp, state[("f", i)], scale=1.0 / 16)
                t1 = TT(F(51 + i), Dm[i], F(27 + i), ALU.mult, t, prevm)
                v3 = bs(i, 16, 528).rearrange("p (a b) -> p a b", b=64)
                t2 = copyA(sm[:, 8 * i:8 * i + 8].unsqueeze(2), v3[:, :, 63:64], t)
                t2 = A(sm[:, 8 * i:8 * i + 8], sm[:, 8 * i:8 * i + 8], ACT.Exp, t2, scale=1.0 / 16)
                tqh.append(t1)
                d3 = Dm[i].rearrange("p (a b) -> p a b", b=64)
                ref = v3[:, :, 63:64].to_broadcast([P, 8, 64])
                t = TT(d3, v3, ref, ALU.subtract, t1, t2)
                t = A(Dm[i], Dm[i], ACT.Exp, t, scale=-1.0 / 16)
                t = TT(F(57 + i), Dm[i], k_ap(i)[:, 16:528], ALU.mult, t, prevm)
                tm1 = TT(sm[:, 32 + 16 * i:48 + 16 * i], bs(i, 0, 16), bs(i, 15, 16).to_broadcast([P, 16]), ALU.subtract, tb)
                tm1 = A(sm[:, 32 + 16 * i:48 + 16 * i], sm[:, 32 + 16 * i:48 + 16 * i], ACT.Exp, tm1, scale=-1.0 / 16)
                tm1 = TT(sm[:, 32 + 16 * i:48 + 16 * i], sm[:, 32 + 16 * i:48 + 16 * i], k_ap(i)[:, 0:16], ALU.mult, tm1)
                tkh.append([t, tm1, t2])
                yield
            tkt = []
            for i in range(2):
                b = acq(MB)
                for tt in range(4):
                    t = TR(b.ap[:, tt * 128:(tt + 1) * 128], F(57 + i)[:, tt * 128:(tt + 1) * 128], mat("ident"), tkh[i], b.free)
                x = copyA(F(59 + i), b.ap[:, :], t, tkh, tqh)
                rel(MB, b, x)
                b = acq(MB)
                t = TR(b.ap[0:16, 0:128], sm[:, 32 + 16 * i:48 + 16 * i], mat("ident"), b.free)
                y = copyA(khm[:, i * 128:(i + 1) * 128], b.ap[0:16, 0:128], t)
                rel(MB, b, y)
                tkt.append([x, y])
                yield

            def S(c, i):
                z = (c * 2 + i) * 128
                if z < 512 + 512:
                    return ZF[:, 55 * 512 + z:55 * 512 + z + 128]
                return ZF[:, 24 * 512 + (z - 1024):24 * 512 + (z - 1024) + 128]
            b = acq(MB)
            for i in range(2):
                for hh in range(2):
                    h = 2 * i + hh
                    t = MM(b.ap[hh * 64:hh * 64 + 64, i * 128:(i + 1) * 128], khm[:, h * 64:h * 64 + 64],
                           vmeta[:, h * 128:(h + 1) * 128], tkt, tv[4], b.free)
            tS = {}
            for i in range(2):
                tS[(0, i)] = copyA(S(0, i), b.ap[:, i * 128:(i + 1) * 128], t, tkt, tkh, tqh)
            rel(MB, b, tS[(0, 0)], tS[(0, 1)])
            yield
            for c in range(7):
                b = acq(MB)
                r0 = 64 * (c % 2)
                for i in range(2):
                    for hh in range(2):
                        h = 2 * i + hh
                        t = MM(b.ap[hh * 64:hh * 64 + 64, i * 128:(i + 1) * 128],
                               F(59 + i)[r0:r0 + 64, (c // 2) * 128 + hh * 64:(c // 2) * 128 + hh * 64 + 64],
                               F(29 + c // 2)[r0:r0 + 64, h * 128:(h + 1) * 128], tkt, tv, b.free)
                for i in range(2):
                    tS[(c + 1, i)] = STT(S(c + 1, i), S(c, i), sm[:, 8 * i + c:8 * i + c + 1], b.ap[:, i * 128:(i + 1) * 128],
                                         ALU.mult, ALU.add, t, tS[(c, i)], tkh, prevm, tkt)
                rel(MB, b, tS[(c + 1, 0)], tS[(c + 1, 1)])
                yield
            to = []
            OS = [57, 58, 27, 28]
            state["OS"] = OS
            for h in range(4):
                i, hh = h // 2, h % 2
                b = acq(MB)
                for tt in range(4):
                    cs = slice(tt * 128, (tt + 1) * 128)
                    MM(b.ap[:, cs], F(29 + tt)[:, h * 128:(h + 1) * 128], F(62 + 2 * (tt // 2) + hh)[:, (2 * (tt % 2) + i) * 128:(2 * (tt % 2) + i + 1) * 128],
                       tsc, tv, b.free, stop=False)
                    for c in (2 * tt, 2 * tt + 1):
                        t = MM(b.ap[:, c * 64:(c + 1) * 64], S(c, i)[hh * 64:hh * 64 + 64, :],
                               F(51 + i)[hh * 64:hh * 64 + 64, c * 64:(c + 1) * 64], tS[(c, i)], tqh, start=False,
                               stop=(c % 2 == 1))
                x = copyA(F(OS[h]), b.ap[:, :], t, tkt, tqh)
                rel(MB, b, x)
                to.append(x)
                tlast_o = t
                yield
            state["tlast_o"] = tlast_o
            ys = []
            for h in range(4):
                sq = A(F(59), F(OS[h]), ACT.Square, to[h], tlast_o)
                b = acq(MB)
                t = MM(b.ap[:, :], mat("ones128"), F(59), sq, b.free)
                s = A(F(60), b.ap[:, :], ACT.Sqrt, t, ys[-1] if ys else None, bias=eps(0))
                rel(MB, b, s)
                s = RCP(F(60), F(60), s)
                y = STT(F(OS[h]), F(OS[h]), vec("gla_norm", h), F(60), ALU.mult, ALU.mult, s)
                ys.append(y)
                yield
            state["o"] = ys
            state["done_gla"] = ys

        bgg = bg_gla()
        bgs.append(bgg)

        tya = [None] * 8
        for uu in range(2):
            un = wunit("po")
            for j in range(4):
                i = 4 * uu + j

                def ev(p, t, i=i):
                    tya[i] = copyA(F(43 + i), p, t, tmix, pooled)
                    return tya[i]
                tpo = tile_T(un, j, mixed, 512, ev)
        tsr = [None] * 4
        for uu in range(2):
            un = wunit("r")
            for j in range(2):
                i = 2 * uu + j

                def ev(p, t, i=i):
                    x = TT(F(34 + i), p, RSTD, ALU.mult, t, trs, tpo)
                    s = A(F(39 + i), F(34 + i), ACT.Sigmoid, x, tpo)
                    tsr[i] = TT(F(34 + i), F(34 + i), F(39 + i), ALU.mult, s, x, eng="pool")
                    return x
                tile_T(un, j, xs, 512, ev)
        tg = [None, None]
        for uu in range(4):
            un = wunit("ga")
            for j in range(2):
                i = 2 * uu + j

                def ev(p, t, i=i):
                    T = TMP if i % 2 == 0 else TMP2
                    x = TT(T, p, RSTD, ALU.mult, t, trs, tg[i % 2])
                    s = A(T, T, ACT.Sigmoid, x)
                    tya[i] = TT(F(43 + i), F(43 + i), T, ALU.mult, s, tya[i], eng="pool")
                    tg[i % 2] = tya[i]
                    return x
                tile_T(un, j, xs, 512, ev)
        drain_bg()
        OS = state["OS"]
        os_ = []
        for h in range(4):
            t = TT(F(OS[h]), F(OS[h]), F(34 + h), ALU.mult, state["o"][h], tsr[h])
            t = split(R(62 + h), R(29 + h), F(OS[h]), t, state["tlast_o"])
            os_.append((R(62 + h), R(29 + h), t))
        GB = [51, 52, 55, 56, 24, 25, 59, 60]
        tgb = [None] * 8
        for uu in range(4):
            un = wunit("gb")
            for j in range(2):
                i = 2 * uu + j

                def ev(p, t, i=i):
                    x = TT(F(GB[i]), p, RSTD, ALU.mult, t, trs, state["o"], state["tlast_o"])
                    tgb[i] = A(F(GB[i]), F(GB[i]), ACT.Sigmoid, x)
                    return x
                last_gb = tile_T(un, j, xs, 512, ev)
        m_ = []
        for uu in range(2):
            un = wunit("go")
            for j in range(4):
                i = 4 * uu + j

                def ev(p, t, i=i):
                    x = TT(F(GB[i]), p, F(GB[i]), ALU.mult, t, tgb[i])
                    y = TT(F(GB[i]), F(GB[i]), F(43 + i), ALU.add, x, tya[i], eng="pool")
                    s = split(R(8 + i), R(16 + i), F(GB[i]), y, last_gb)
                    m_.append((R(8 + i), R(16 + i), s))
                    return x
                last_go = tile_T(un, j, os_, 512, ev)
        st = Stat(ACC, [TMP, TMP2], free=[trs, tg, trc])
        u2, th = [], [None] * 8
        for uu in range(4):
            un = wunit("wo")
            for j in range(2):
                i = 2 * uu + j

                def ev(p, t, i=i):
                    x = TT(F(i), F(i), p, ALU.add, t, last_gb)
                    th[i] = [x, st.add(F(i), x)]
                    s = split_scaled(R(24 + i), R(32 + i), F(i), vec("norm_ffn", i), x, last_go, m_[7][2], tgb, tsr)
                    th[i].append(s)
                    u2.append((R(24 + i), R(32 + i), s))
                    return x
                last_wo = tile_T(un, j, m_, 512, ev)
        trs = st.rstd(RSTD, free=[tgb])
        hid_free = last_go
        gfg = V[:, NV:NV + 8]
        tgf = TT(gfg, V[:, vcol("norm_final"):vcol("norm_final") + 8], V[:, vcol("norm_gains_2"):vcol("norm_gains_2") + 8],
                 ALU.mult, TV)
        fst = [None, None]
        xs2 = []
        stA = Stat(F(60), [F(61), F(62)], free=[last_go, last_wo])
        stB = Stat(ACC, [TMP, TMP2], free=st.done)
        stB.t = [st.done]
        for g_ in range(4):
            hs = []
            for uu in range(4):
                un = wunit("f1")
                for j in range(2):
                    i = 2 * uu + j

                    def ev(p, t, i=i, hid_free=hid_free):
                        T = F(56 + i % 2)
                        T2 = F(58 + i % 2)
                        x = STT(T, p, 0.0, RSTD, ALU.max, ALU.mult, t, trs, fst[i % 2], tgb)
                        y = A(T2, T, ACT.Square, x, fst[i % 2])
                        s = split(R(40 + i), R(48 + i), T2, y, hid_free, eng="pool")
                        fst[i % 2] = s
                        hs.append((R(40 + i), R(48 + i), s))
                        return x
                    tile_T(un, j, u2, 512, ev)
            for uu in range(4):
                un = wunit("f2")
                for j in range(2):
                    i = 2 * uu + j

                    def ev(p, t, i=i, g_=g_):
                        x = TT(F(i), F(i), p, ALU.add, t, th[i])
                        th[i] = [x]
                        if g_ == 3:
                            th[i].append(stA.add(F(i), x))
                            th[i].append(stB.add(F(i), x, scale=vec("norm_final", i)))
                            s = split_scaled(R(8 + i), R(16 + i), F(i), gfg[:, i:i + 1], x, tgf, last_wo)
                            th[i].append(s)
                            xs2.append((R(8 + i), R(16 + i), s))
                        return x
                    hid_free = tile_T(un, j, hs, 512, ev)
        RA = F(63)
        tra = stA.rstd(RA, free=hid_free)
        b, t = stB.mean()
        x = TT(RSTD, b.ap[:, :], RA, ALU.mult, t, tra, fst)
        rel(DB, b, x)
        x = TT(RSTD, RSTD, RA, ALU.mult, x)
        x = A(RSTD, RSTD, ACT.Sqrt, x, bias=eps(0))
        x = RCP(RSTD, RSTD, x)
        trs = TT(RSTD, RSTD, RA, ALU.mult, x)
        stb_done = t
        tx = [STT(F(i), F(i), vec("norm_final", i), RA, ALU.mult, ALU.mult, tra, th[i]) for i in range(8)]

        wau_sb, gupg_sb = F(40), F(41)
        tw1 = dma("wau", wau_sb, wau, hid_free)
        tw2 = dma("gupg", gupg_sb, gupg, hid_free)
        ZB = [ZF[:, 42 * 512 + 520 * i:42 * 512 + 520 * i + 513] for i in range(2)]
        zfree = [dve(lambda e, i=i: e.memset(ZB[i][:, 0:1], 0.0), hid_free) for i in range(2)]
        zc = [0]
        dst_of = {}
        order = [12, 13]
        for i in range(4):
            order += [4 + i, i]
            if i % 2:
                order += [8 + i - 1, 8 + i]
        slot_of = {**{i: 24 + i for i in range(12)}, 12: 36, 13: 37}
        tp = {}
        oi = 0
        last_f1 = hid_free
        for uu in range(7):
            un = wunit("p")
            for j in range(2):
                f = order[oi]
                oi += 1

                def ev(p, t, f=f):
                    z = ZB[zc[0] % 2]
                    zi = zc[0] % 2
                    zc[0] += 1
                    dd = F(45 + zi)
                    x = TT(z[:, 1:513], p, RSTD, ALU.mult, t, trs, zfree[zi])
                    y = TT(dd, z[:, 0:512], z[:, 1:513], ALU.subtract, x, zfree[zi], hid_free, eng="pool")
                    w = STT(F(slot_of[f]), dd, vec("mu_first_2", f), z[:, 1:513], ALU.mult, ALU.add, y, x, last_f1)
                    zfree[zi] = [w, y]
                    if f == 12:
                        w = A(F(36)[0:64, :], F(36)[0:64, :], ACT.Tanh, w)
                    if f == 13:
                        w = A(F(37), F(37), ACT.Sigmoid, w)
                    tp[f] = w
                    return x
                tile_T(un, j, xs2, 512, ev)

        yr = [None] * 4
        rw = {"hp": None, "px": None}

        def head_gen(hp, hh, base, fr, res):
            r0 = 64 * hh
            RT, PK, QT, AT, AA, Z, T, X1, M1, M2 = [F(base[i]) for i in range(10)]
            PX, GH = F(base[10]), F(base[11])

            def v4(x):
                return x.rearrange("p (a b) -> p a b", b=128)

            def prod(lhs, rhs):
                b = acq(MB)
                for tt in range(4):
                    cs = slice(tt * 128, (tt + 1) * 128)
                    t = MM(b.ap[:, cs], lhs[r0:r0 + 64, cs], rhs[r0:r0 + 64, cs], b.free, fr["in"])
                return b, t
            ro, Pp, nB, Kk = fr["ro"], fr["P"], fr["nB"], fr["K"]
            b, t = prod(nB, Pp)
            tAT = TT(v4(AT), v4(b.ap[:, :]), mask4("lt"), ALU.mult, t, fr["free"])
            rel(MB, b, tAT)
            b, t = prod(Pp, nB)
            tAA = copyA(AA, b.ap[:, :], t, fr["free"])
            rel(MB, b, tAA)
            yield
            tm1 = TT(v4(Z), v4(AT), mask4("u0"), ALU.mult, tAT)
            tZ = TT(v4(Z), v4(Z), mat("ident").unsqueeze(1).to_broadcast([P, 4, 128]), ALU.add, tm1, TCF)
            tm1 = TT(v4(T), v4(AA), mask4("l0"), ALU.mult, tAA, TCU)
            tT = TT(v4(T), v4(T), mat("ident").unsqueeze(1).to_broadcast([P, 4, 128]), ALU.add, tm1)
            yield
            b, t = prod(Kk, Pp)
            tPK = TT(v4(PK), v4(b.ap[:, :]), mask4("lt"), ALU.mult, t)
            rel(MB, b, tPK)
            b, t = prod(Kk, ro)
            tRT = TT(v4(RT), v4(b.ap[:, :]), mask4("le"), ALU.mult, t)
            rel(MB, b, tRT)
            b, t = prod(nB, ro)
            tQT = TT(v4(QT), v4(b.ap[:, :]), mask4("le"), ALU.mult, t)
            rel(MB, b, tQT)
            yield
            b = acq(MB)
            for tt in range(4):
                t = MM(b.ap[:, tt * 64:(tt + 1) * 64], PK[:, tt * 128:(tt + 1) * 128],
                       fr["Vt"][:, tt * 128 + r0:tt * 128 + r0 + 64], tPK, b.free, fr["in"])
            px3 = v4(PX)
            tX = copyA(px3[:, :, 64:128], b.ap[:, 0:256].rearrange("p (a b) -> p a b", b=64), t, fr["free"])
            rel(MB, b, tX)
            tX2 = copyA(px3[:, :, 0:64], v4(fr["Pt"])[:, :, r0:r0 + 64], fr["in"])
            fr["ptfree"].append(tX2)
            yield
            tX1 = None
            tl = None
            for l in range(1, 6):
                tmm = TT(v4(M1), v4(AA), mask4(f"l{l}"), ALU.mult, tAA, tl, eng="dve")
                b = acq(MB)
                for tt in range(4):
                    cs = slice(tt * 128, (tt + 1) * 128)
                    t = MM(b.ap[:, cs], M1[:, cs], Z[:, cs], tmm, tZ, b.free)
                tX1 = copyA(X1, b.ap[:, :], t, tl)
                tl1 = t
                rel(MB, b, tX1)
                yield
                b = acq(MB)
                for tt in range(4):
                    cs = slice(tt * 128, (tt + 1) * 128)
                    t = MM(b.ap[:, cs], T[:, cs], X1[:, cs], tX1, tT, b.free)
                if l < 5:
                    b2 = acq(MB)
                    for tt in range(4):
                        cs = slice(tt * 128, (tt + 1) * 128)
                        t2 = MM(b2.ap[:, cs], X1[:, cs], T[:, cs], tX1, tT, b2.free)
                tZ = TT(Z, Z, b.ap[:, :], ALU.add, t, tZ)
                rel(MB, b, tZ)
                tl = [t, tl1]
                if l < 5:
                    tT = TT(T, T, b2.ap[:, :], ALU.add, t2, tT)
                    rel(MB, b2, tT)
                    tl = [t2, tl1]
                yield
            b = acq(MB)
            for tt in range(4):
                cs = slice(tt * 128, (tt + 1) * 128)
                t = MM(b.ap[:, cs], Z[:, cs], PX[:, cs], tZ, tX, tX2, b.free)
            tGH = copyA(GH, b.ap[:, :], t)
            rel(MB, b, tGH)
            res.update(GH=GH, tGH=tGH, QT=QT, tQT=tQT, RT=RT, tRT=tRT)
            yield

        def bg_rwkv():
            TA, TB, TC, TD = F(58), F(59), F(60), F(61)
            prev_all = [tx, trs]
            hfree = [None, None]
            for hp in range(4):
                r_, k_, v_ = F(24 + hp), F(28 + hp), F(32 + hp)
                ro, Pp, nB, Kk = F(47), F(48), F(49), F(50)
                nBt, Kt, Vt, Pt = F(51), F(52), F(53), F(54)
                BV = F(55)
                sg, at = TA, TB
                b = acq(MB)
                t = MM(b.ap[:, :], wau_sb[0:64, hp * 128:(hp + 1) * 128], F(36)[0:64, :], tp[12], tw1, b.free)
                b2 = acq(MB)
                t2 = MM(b2.ap[:, :], wau_sb[64:128, hp * 128:(hp + 1) * 128], F(36)[64:128, :], b2.free)
                x = A(sg, b.ap[:, :], ACT.Sigmoid, t, prev_all, bias=vec("w0_2", hp))
                rel(MB, b, x)
                y = A(at, b2.ap[:, :], ACT.Sigmoid, t2, prev_all, bias=vec("a0_2", hp))
                rel(MB, b2, y)
                bb = TC
                tb = dve(lambda e: e.tensor_tensor_scan(bb, RS512, sg, 0.0, ALU.mult, ALU.add), x, TCU, prev_all)
                b3 = bb.rearrange("p (a b) -> p a b", b=64)
                mid = b3[:, :, 31:32]
                dsm = sm[:, 0:8]
                z = TT(dsm.unsqueeze(2), b3[:, :, 63:64], mid, ALU.subtract, tb, rw["hp"])
                z = TT(dsm[:, 0:7].unsqueeze(2), dsm[:, 0:7].unsqueeze(2), b3[:, 1:8, 31:32], ALU.add, z)
                tD = A(dsm, dsm, ACT.Exp, z, scale=-DECAY)
                tdd = TT(TD.rearrange("p (a b) -> p a b", b=64), b3, mid.to_broadcast([P, 8, 64]), ALU.subtract, tb,
                         prev_all)
                yield
                kkv = F(62)
                q1 = TS(kkv, k_, vec("k_k_2", hp), ALU.mult, tp[4 + hp], prev_all)
                q2 = A(F(63), kkv, ACT.Square, q1, prev_all)
                b = acq(MB)
                t = MM(b.ap[:, :], mat("blk"), F(63), q2, b.free)
                q3 = TS(F(63), b.ap[:, :], 1e-24, ALU.max, t)
                rel(MB, b, q3)
                q3 = A(F(63), F(63), ACT.Sqrt, q3)
                q3 = RCP(F(63), F(63), q3)
                tkk = TT(kkv, kkv, F(63), ALU.mult, q3)
                yield
                q4 = TS(F(63), at, 1.0, ALU.subtract, y, tkk, s2=vec("k_a_2", hp), o2=ALU.mult)
                tkp = STT(F(64), F(63), 1.0, k_, ALU.add, ALU.mult, q4, tp[4 + hp])
                e1 = A(Pp, TD, ACT.Exp, tdd, prev_all, scale=-DECAY)
                tro = TT(ro, r_, Pp, ALU.mult, e1, tp[hp], prev_all, eng="pool")
                e2 = A(Kk, TD, ACT.Exp, tdd, prev_all, scale=DECAY)
                e3 = TT(nB, kkv, at, ALU.mult, tkk, y, prev_all)
                tnB = STT(nB, nB, -1.0, Kk, ALU.mult, ALU.mult, e3, e2)
                tKk = TT(Kk, F(64), Kk, ALU.mult, tkp, tnB)
                e4 = TT(TD, TD, sg, ALU.subtract, e1, e2, tdd)
                e4 = A(TD, TD, ACT.Exp, e4, scale=-DECAY)
                tP = TT(Pp, kkv, TD, ALU.mult, e4, tro, tkk)
                yield
                q5 = STT(F(63), r_, vec("r_k_2", hp), F(64), ALU.mult, ALU.mult, tkp, tp[hp])
                b = acq(MB)
                t = MM(b.ap[:, :], mat("blk"), F(63), q5, b.free)
                tBV = TT(BV, b.ap[:, :], v_, ALU.mult, t, tp[8 + hp], rw["hp"])
                rel(MB, b, tBV)
                ttr = []
                for src, dst, tk in ((nB, nBt, tnB), (Kk, Kt, tKk), (v_, Vt, tp[8 + hp]), (Pp, Pt, tP)):
                    b = acq(MB)
                    for tt in range(4):
                        cs = slice(tt * 128, (tt + 1) * 128)
                        t = TR(b.ap[:, cs], src[:, cs], mat("ident"), tk, b.free)
                    x = copyA(dst, b.ap[:, :], t, prev_all)
                    rel(MB, b, x)
                    ttr.append(x)
                    yield
                fin_ = [tro, tP, tnB, tKk] + ttr
                res = [{}, {}]
                gens = []
                ptf = []
                bases = [[8, 9, 10, 11, 12, 13, 14, 15, 16, 17, 18, 19], [20, 21, 22, 23, 56, 57, 58, 59, 60, 61, 62, 63]]
                for hh in range(2):
                    fr = {"in": fin_, "ro": ro, "P": Pp, "nB": nB, "K": Kk, "Vt": Vt, "Pt": Pt, "ptfree": ptf,
                          "free": [state["last_cv"], hfree, tBV, tP, tD, fin_, q5, tBV]}
                    gens.append(head_gen(hp, hh, bases[hh], fr, res[hh]))
                live = list(gens)
                while live:
                    for g2 in list(live):
                        try:
                            next(g2)
                        except StopIteration:
                            live.remove(g2)
                    yield
                Y1 = F(17)
                b = acq(MB)
                for hh in range(2):
                    r0 = 64 * hh
                    for tt in range(4):
                        cs = slice(tt * 128, (tt + 1) * 128)
                        t = MM(b.ap[r0:r0 + 64, cs], res[hh]["GH"][:, tt * 128:tt * 128 + 64], res[hh]["QT"][:, cs],
                               res[hh]["tGH"], res[hh]["tQT"], b.free)
                tY1 = TT(Y1, b.ap[:, :], ro, ALU.add, t, [res[0]["tGH"], res[1]["tGH"]])
                rel(MB, b, tY1)
                M2 = F(16)
                bb_ = [acq(MB), acq(MB)]
                tl = []
                for par in range(2):
                    c0 = 64 * par
                    n2 = 4 - par
                    for hh in range(2):
                        r0 = 64 * hh
                        for a_ in range(n2):
                            t = MM(bb_[par].ap[r0:r0 + 64, a_ * 64:(a_ + 1) * 64],
                                   res[hh]["GH"][c0:c0 + 64, a_ * 128:a_ * 128 + 64],
                                   nBt[c0:c0 + 64, a_ * 128 + r0:a_ * 128 + r0 + 64], bb_[par].free)
                    one = []
                    for hh in range(2):
                        r0 = 64 * hh
                        idn = mat("ident")[r0:r0 + 64, r0:r0 + 64].unsqueeze(1).to_broadcast([64, n2, 64])
                        mv = M2[r0:r0 + 64, :].rearrange("p (a two b) -> p two a b", two=2, b=64)[:, par, 0:n2, :]
                        one.append(TT(mv, bb_[par].ap[r0:r0 + 64, 0:64 * n2].rearrange("p (a b) -> p a b", b=64), idn,
                                      ALU.add, t, tY1))
                    rel(MB, bb_[par], one)
                    tl += one
                yield
                ND = F(13)
                bb_ = [acq(MB), acq(MB)]
                tN = []
                for par in range(2):
                    c0 = 64 * par
                    n2 = 4 - par
                    for hh in range(2):
                        r0 = 64 * hh
                        for a_ in range(n2):
                            kc = slice(a_ * 128 + r0, a_ * 128 + r0 + 64)
                            o_ = bb_[par].ap[r0:r0 + 64, a_ * 64:(a_ + 1) * 64]
                            MM(o_, Kt[c0:c0 + 64, kc], Vt[c0:c0 + 64, kc], bb_[par].free, stop=False)
                            t = MM(o_, nBt[c0:c0 + 64, kc], res[hh]["GH"][c0:c0 + 64, a_ * 128 + 64:a_ * 128 + 128],
                                   start=False)
                    nv = ND.rearrange("p (a two b) -> p two a b", two=2, b=64)[:, par, 0:n2, :]
                    dv = dsm.rearrange("p (a two) -> p two a", two=2)[:, par, 0:n2].unsqueeze(2).to_broadcast([P, n2, 64])
                    x = TT(nv, bb_[par].ap[:, 0:64 * n2].rearrange("p (a b) -> p a b", b=64), dv, ALU.mult, t, tD, tY1)
                    rel(MB, bb_[par], x)
                    tN.append(x)
                yield
                SS = F(15)
                tS = dve(lambda e: e.memset(SS[:, 0:64], 0.0), tl)
                tS = [tS, dve(lambda e: e.tensor_copy(SS[:, 64:128], ND[:, 0:64]), tN, tl)]
                for c in range(1, 7):
                    b = acq(MB)
                    for hh in range(2):
                        r0 = 64 * hh
                        t = MM(b.ap[r0:r0 + 64, 0:64], M2[r0:r0 + 64, c * 64:(c + 1) * 64],
                               SS[r0:r0 + 64, c * 64:(c + 1) * 64], b.free, tS, tl)
                    tS = STT(SS[:, (c + 1) * 64:(c + 2) * 64], b.ap[:, 0:64], dsm[:, c:c + 1],
                             ND[:, c * 64:(c + 1) * 64], ALU.mult, ALU.add, t, tD, tN)
                    rel(MB, b, tS)
                    yield
                rw["hp"] = tS
                b = acq(MB)
                for hh in range(2):
                    r0 = 64 * hh
                    for tt in range(4):
                        cs = slice(tt * 128, (tt + 1) * 128)
                        o_ = b.ap[r0:r0 + 64, cs]
                        MM(o_, Vt[:, tt * 128 + r0:tt * 128 + r0 + 64], res[hh]["RT"][:, cs], b.free, res[hh]["tRT"],
                           stop=False)
                        MM(o_, res[hh]["GH"][:, tt * 128 + 64:tt * 128 + 128], res[hh]["QT"][:, cs], start=False, stop=False)
                        for c in (2 * tt, 2 * tt + 1):
                            t = MM(b.ap[r0:r0 + 64, c * 64:(c + 1) * 64], SS[r0:r0 + 64, c * 64:(c + 1) * 64],
                                   Y1[r0:r0 + 64, c * 64:(c + 1) * 64], tS, tY1, start=False, stop=(c % 2 == 1))
                yy, T1, T2 = F(14), F(13), F(12)
                ty = copyA(yy, b.ap[:, :], t)
                rel(MB, b, ty)
                tlastY = t
                yield
                b = acq(MB)
                t = MM(b.ap[:, :], mat("blk64"), yy, ty, b.free)
                t1_ = TT(yy, yy, b.ap[:, :], ALU.subtract, t)
                rel(MB, b, t1_)
                t2_ = A(T1, yy, ACT.Square, t1_, t)
                b = acq(MB)
                t = MM(b.ap[:, :], mat("blk64"), T1, t2_, b.free)
                t3_ = A(T2, b.ap[:, :], ACT.Sqrt, t, bias=eps(2))
                rel(MB, b, t3_)
                t3_ = RCP(T2, T2, t3_)
                t4_ = STT(yy, yy, vec("lnx_g_2", hp), T2, ALU.mult, ALU.mult, t3_, t1_)
                t4_ = STT(yy, yy, vec("lnx_b_2", hp), BV, ALU.add, ALU.add, t4_, tBV)
                b = acq(MB)
                t = MM(b.ap[:, :], gupg_sb[:, hp * 128:(hp + 1) * 128], F(37), tp[13], tw2, b.free)
                t4_ = TT(yy, yy, b.ap[:, :], ALU.mult, t4_, t)
                rel(MB, b, t4_)
                s = split(R(24 + hp), R(28 + hp), yy, t4_)
                yr[hp] = (R(24 + hp), R(28 + hp), s)
                prev_all = [tlastY, t, s, tS]
                hfree = [tlastY, s]
                rw["hp"] = [tS, t4_]
                yield

        ZC = [ZF[:, 38 * 512:38 * 512 + 542], ZF[:, 42 * 512:42 * 512 + 542],
              ZF[:, 42 * 512 + 542:42 * 512 + 1084], ZF[:, 45 * 512:45 * 512 + 542]]
        tcz = []
        for i in range(4):
            tcz.append(dve(lambda e, i=i: e.memset(ZC[i][:, 0:30], 0.0), zfree, last_f1))
        thc = [None] * 4
        for i in range(4):
            un = wunit("cv")

            def ev(p, t, i=i):
                x = TT(ZC[i][:, 30:542], p, RSTD, ALU.mult, t, trs, zfree)
                thc[i] = x
                return x
            tile_T(un, 0, xs2, 512, ev)

            def ev(p, t, i=i):
                T = F(67 + 2 * (i % 2))
                x = TT(T, p, RSTD, ALU.mult, t, trs, state.get(("cg", i % 2)), stA.t, stB.t, tra, hid_free)
                s = A(T, T, ACT.Sigmoid, x)
                thc[i] = TT(ZC[i][:, 30:542], ZC[i][:, 30:542], T, ALU.mult, s, thc[i])
                state[("cg", i % 2)] = thc[i]
                return x
            state["last_cv"] = tile_T(un, 1, xs2, 512, ev)
            if i == 0:
                bgs.append(bg_rwkv())
        last_cv = state["last_cv"]
        CO = [F(65), F(66), F(67), F(69)]
        cvres = []

        def bg_conv():
            tc = [None] * 4
            for i in range(4):
                for tap in range(31):
                    w = V[:, vcol("conv_w_2") + tap * 4 + i:vcol("conv_w_2") + tap * 4 + i + 1]
                    src = ZC[i][:, tap:tap + 512]
                    if tap == 0:
                        tc[i] = TS(CO[i], src, w, ALU.mult, thc[i], tcz, trs, stb_done, tra, tx, s2=vec("conv_b_2", i),
                                   o2=ALU.add)
                    else:
                        tc[i] = STT(CO[i], src, w, CO[i], ALU.mult, ALU.add, tc[i])
                    if tap % 2:
                        yield
            b = acq(DB)
            for i in range(4):
                t = MM(b.ap[:, :], mat("ones512"), CO[i], tc[i], b.free, start=(i == 0), stop=(i == 3))
            mt = []
            for i in range(4):
                mt.append(TT(CO[i], CO[i], b.ap[:, :], ALU.subtract, t))
            rel(DB, b, mt)
            yield
            b = acq(DB)
            SQ = F(38)
            sqt = None
            for i in range(4):
                s = A(SQ, CO[i], ACT.Square, mt[i], sqt, trs, last_cv, thc)
                sqt = MM(b.ap[:, :], mat("ones512"), SQ, s, b.free, start=(i == 0), stop=(i == 3))
            s = A(F(39), b.ap[:, :], ACT.Sqrt, sqt, bias=eps(1))
            rel(DB, b, s)
            s = RCP(F(39), F(39), s)
            yield
            for i in range(4):
                x = STT(CO[i], CO[i], vec("conv_ln_g_2", i), F(39), ALU.mult, ALU.mult, s, mt[i])
                x = TS(CO[i], CO[i], vec("conv_ln_b_2", i), ALU.add, x)
                g_ = A(SQ, CO[i], ACT.Sigmoid, x, cvres[-1][3] if cvres else None, sqt)
                x = TT(CO[i], CO[i], SQ, ALU.mult, g_)
                hi, lo = [(R(42), R(43)), (R(44), R(45)), (R(46), R(68)), (R(65), R(66))][i]
                y = split(hi, lo, CO[i], x, tc, [c[2] for c in cvres])
                cvres.append((hi, lo, y, x))
                yield

        bgs.append(bg_conv())
        drain_bg()
        cat = [(c[0], c[1], c[2]) for c in cvres] + yr

        def nexp(n):
            return [p_[2] for p_ in n]

        def residual(ys, yt, gi, tx, statA, nxt_slots, nxt_g, wfree, stat_next):
            t = statA.rstd(RSTD, free=wfree)
            outp = []
            for i in range(8):
                a = STT(ys[i], ys[i], vec("norm_gains_2", 8 * gi + i), RSTD, ALU.mult, ALU.mult, t, yt[i])
                tx[i] = TT(F(i), F(i), ys[i], ALU.add, a, tx[i], eng="pool" if i % 2 else "dve")
                if nxt_g is not None:
                    q_ = stat_next.add(F(i), tx[i])
                    hi, lo = nxt_slots[i]
                    s = split_scaled(hi, lo, F(i), vec("norm_gains_2", 8 * nxt_g + i), tx[i], wfree)
                    outp.append((hi, lo, s))
            return outp

        YS = [F(47 + i) for i in range(8)]
        RW = yr[3][2]
        allrw = [p_[2] for p_ in yr]
        stat = Stat(F(55), [F(56), F(57)], free=[allrw])
        yt = [None] * 8
        for uu in range(4):
            un = wunit("wo2")
            for j in range(2):
                i = 2 * uu + j

                def ev(p, t, i=i):
                    x = copyA(YS[i], p, t, allrw)
                    yt[i] = [x, stat.add(YS[i], x)]
                    return x
                last_o2 = tile_T(un, j, cat, 512, ev)
        mraw = F(59, 2048)
        tmr = dma("mem", mraw.rearrange("p (k t) -> p k t", t=256), memT.rearrange("(k p) t -> p k t", p=P), allrw)
        mst = Stat(F(69)[:, 0:256], [F(69)[:, 256:512]], 256, free=[last_o2, allrw])
        mx = []
        for k in range(8):
            src = mraw[:, k * 256:(k + 1) * 256]
            ks = slice((k % 2) * 256, (k % 2) * 256 + 256)
            hi, lo = R(32 + k // 2)[:, ks], R(8 + k // 2)[:, ks]
            s = split_scaled(hi, lo, src, vec("mem_norm_g_2", k), tmr, allrw)
            mst.add(src, tmr)
            mx.append((hi, lo, s))
        MR = F(63)[:, 0:256]
        tmrs = mst.rstd(MR, free=[allrw])
        b = acq(DB)
        for i in range(2):
            t = MM(b.ap[:, i:i + 1], mst.acc[:, i * 128:(i + 1) * 128], mat("ones1024")[:, 0:1], b.free)
        t = A(rcol[:, 0:2], b.ap[:, 0:2], ACT.Sqrt, t, bias=eps(0))
        rel(DB, b, t)
        tmc = RCP(rcol[:, 0:2], rcol[:, 0:2], t)
        st3 = Stat(F(58), [F(56), F(57)], free=[allrw, stat.t])
        xs3 = residual(YS, yt, 1, tx, stat, [(R(12 + i), R(20 + i) if i < 4 else R(24 + i)) for i in range(8)], 2,
                       [last_o2, allrw, last_cv], st3)
        trs3 = st3.rstd(RSTD, free=[tx])
        km_ap = []
        for i in range(8):
            s0 = 42 * 512 if i < 4 else 38 * 512
            if i >= 6:
                s0 = 44 * 512
                km_ap.append(ZF[:, s0 + (i - 6) * 256:s0 + (i - 5) * 256])
            elif i >= 4:
                km_ap.append(ZF[:, s0 + (i - 4) * 256:s0 + (i - 3) * 256])
            else:
                km_ap.append(ZF[:, s0 + i * 256:s0 + (i + 1) * 256])
        tkm = [None] * 8
        for uu in range(4):
            un = wunit("km")
            for j in range(2):
                i = 2 * uu + j

                def ev(p, t, i=i):
                    tkm[i] = TT(km_ap[i], p, MR, ALU.mult, t, tmrs, last_o2)
                    return tkm[i]
                tile_T(un, j, mx, 256, ev)
        vm_ap = [[None] * 4, [None] * 4]
        vslots = [64, 65, 45, 46]
        for mt in range(2):
            for c in range(4):
                s0 = vslots[2 * mt + c // 2] * 512 + (c % 2) * 256
                vm_ap[mt][c] = ZF[:, s0:s0 + 256]
        tvm = []
        for uu in range(4):
            un = wunit("vm")
            for mt in range(2):
                def ev(p, t, uu=uu, mt=mt):
                    x = TS(vm_ap[mt][uu], p, rcol[:, mt:mt + 1], ALU.mult, t, tmc, last_o2)
                    tvm.append(x)
                    return x
                tile_M(un, mx, mt * 128, 128, ev)
        tqq = [None] * 8
        for uu in range(4):
            un = wunit("wq")
            for j in range(2):
                i = 2 * uu + j

                def ev(p, t, i=i):
                    tqq[i] = STT(F(47 + i), p, 1.0 / 16, RSTD, ALU.mult, ALU.mult, t, trs3, tx)
                    return tqq[i]
                last_q = tile_T(un, j, xs3, 512, ev)
        ao = []
        prf = [None, None]
        ptfree = [None, None]
        for h in range(4):
            z = h % 2
            PR = F(56 + 2 * z, 1024)
            PT = [F(60 + 2 * z), F(61 + 2 * z)]
            tpr = []
            for tt in range(4):
                b = acq(MB)
                for d in range(2):
                    t = MM(b.ap[:, 0:256], F(47 + 2 * h + d)[:, tt * 128:(tt + 1) * 128], km_ap[2 * h + d], tqq, tkm,
                           b.free, start=(d == 0), stop=(d == 1))
                c = 16 * z + 4 * tt
                nm, ssum = sm[:, c:c + 1], sm[:, c + 1:c + 2]
                pr = PR[:, tt * 256:(tt + 1) * 256]
                x = dve(lambda e, nm=nm, b=b: e.tensor_reduce(nm, b.ap[:, 0:256], mybir.AxisListType.X, ALU.max,
                                                            negate=True), t, prf[z], rw["hp"], st3.done)
                y = act(lambda e, pr=pr, b=b, nm=nm, ssum=ssum: e.activation(pr, b.ap[:, 0:256], ACT.Exp, bias=nm,
                                                                            scale=1.0, accum_out=ssum),
                        x, prf[z], ptfree[z], trs3, tmrs, tx)
                rel(MB, b, y)
                w = RCP(ssum, ssum, y)
                w = TS(pr, pr, ssum, ALU.mult, w, y)
                tpr.append(w)
            tt_ = []
            for mt in range(2):
                b = acq(MB)
                for tt in range(4):
                    t = TR(b.ap[:, tt * 128:(tt + 1) * 128], PR[:, tt * 256 + mt * 128:tt * 256 + mt * 128 + 128],
                           mat("ident"), tpr, b.free)
                x = copyA(PT[mt], b.ap[:, :], t, ptfree[z], tmrs, tkm, tvm)
                rel(MB, b, x)
                tt_.append(x)
            prf[z] = [t]
            for d in range(2):
                b = acq(MB)
                for mt in range(2):
                    t = MM(b.ap[:, :], vm_ap[mt][h][:, d * 128:(d + 1) * 128], PT[mt], tt_, tvm, b.free,
                           start=(mt == 0), stop=(mt == 1))
                i = 2 * h + d
                hi, lo = (R(32 + i) if i < 4 else R(4 + i), R(24 + i) if i < 4 else R(38 + i - 4) if i < 6 else R(66 + i - 6))
                s = split(hi, lo, b.ap[:, :], t, last_q, tvm, tkm)
                rel(MB, b, s)
                ao.append((hi, lo, s))
            ptfree[z] = [t]
        last_att = t
        stat = Stat(F(56), [F(57), F(58)], free=[last_att, tpr])
        yt = [None] * 8
        for uu in range(4):
            un = wunit("xo")
            for j in range(2):
                i = 2 * uu + j

                def ev(p, t, i=i):
                    x = copyA(YS[i], p, t, last_att)
                    yt[i] = [x, stat.add(YS[i], x)]
                    return x
                last_xo = tile_T(un, j, ao, 512, ev)
        st4 = Stat(F(59), [F(60), F(61)], free=[last_att])
        xs4 = residual(YS, yt, 3, tx, stat, [(R(24 + i), R(32 + i)) for i in range(8)], 4, [last_xo], st4)
        trs4 = st4.rstd(RSTD, free=[tx])
        fst = [None, None]
        dn_free = last_xo
        AC = [F(40 + i) for i in range(8)]
        tac = [None] * 8
        stat = Stat(F(58), [F(60), F(61)], free=[st4.done])
        for g_ in range(3):
            nt = 8 if g_ < 2 else 6
            hs = []
            for i in range(nt):
                un = wunit("gu")
                T, T2 = F(48 + i % 2), F(50 + i % 2)

                def ev(p, t, i=i, T=T, T2=T2):
                    x = TT(T, p, RSTD, ALU.mult, t, trs4, fst[i % 2], tx)
                    y = A(T2, T, ACT.Sigmoid, x, fst[i % 2])
                    y = TT(T, T, T2, ALU.mult, x, y, eng="pool")
                    fst[i % 2] = y
                    return x
                tile_T(un, 0, xs4, 512, ev)

                def ev(p, t, i=i, T=T, T2=T2, dn_free=dn_free):
                    x = TT(T2, p, RSTD, ALU.mult, t, fst[i % 2])
                    y = TT(T, T, T2, ALU.mult, x, fst[i % 2], eng="pool")
                    s = split(R(8 + i), R(16 + i), T, y, dn_free, eng="pool")
                    fst[i % 2] = s
                    hs.append((R(8 + i), R(16 + i), s))
                    return x
                tile_T(un, 1, xs4, 512, ev)
            for uu in range(4):
                un = wunit("dn")
                for j in range(2):
                    i = 2 * uu + j

                    def ev(p, t, i=i, g_=g_):
                        if g_ == 0:
                            x = copyA(AC[i], p, t, last_xo, tx)
                            tac[i] = x
                        else:
                            x = TT(AC[i], AC[i], p, ALU.add, t, tac[i])
                            tac[i] = x
                        if g_ == 2:
                            tac[i] = [x, stat.add(AC[i], x)]
                        return x
                    dn_free = tile_T(un, j, hs, 512, ev)
        t = stat.rstd(RSTD, free=[fst])
        ov = out.rearrange("(k p) t -> p k t", p=P)
        outs = []
        for i in range(8):
            a = STT(AC[i], AC[i], vec("norm_gains_2", 40 + i), RSTD, ALU.mult, ALU.mult, t, tac[i])
            a = TT(F(i), F(i), AC[i], ALU.add, a, tx[i])
            outs.append(dma("out", ov[:, i, :], F(i), a))
        op("sp", None, outs)

        for n in names[:4]:
            c = 0
            for after, fn, tok in Q[n]:
                if tok.used:
                    c += 1
                    tok.sem, tok.val = esem[n], c

        def run(eng, n):
            seen = {}
            for after, fn, tok in Q[n]:
                need = {}
                for t in after:
                    if n == "pe" and t.eng == "pe":
                        continue
                    k = t.sem.name
                    if t.val > need.get(k, (0, None))[0]:
                        need[k] = (t.val, t.sem)
                for k, (v, s) in need.items():
                    if v > seen.get(k, 0):
                        eng.wait_ge(s, v)
                        seen[k] = v
                if fn is None:
                    continue
                ins = fn(eng)
                if tok.eng == "dma":
                    ins.then_inc(tok.sem, 16)
                elif tok.used:
                    ins.then_inc(tok.sem, 1)

        block = ctx.enter_context(nc.Block())

        @block.sync
        def _(eng):
            run(eng, "sp")

        @block.tensor
        def _(eng):
            run(eng, "pe")

        @block.scalar
        def _(eng):
            run(eng, "act")

        @block.vector
        def _(eng):
            run(eng, "dve")

        @block.gpsimd
        def _(eng):
            run(eng, "pool")


def lay_out(inputs):
    import numpy as np
    I = {k: np.asarray(v) for k, v in inputs.items()}
    flat = []
    for tag, w, r0, nk, cols, width, kind in unit_list():
        W = I[w].reshape(I[w].shape[-2], I[w].shape[-1])[r0:r0 + nk * 128]
        if kind == "T":
            x = np.stack([W[:, c:c + width].reshape(nk, 128, width) for c in cols], 0)
            x = x.transpose(2, 0, 1, 3)
        else:
            x = W[:, cols[0]:cols[0] + width].reshape(nk, 128, width).transpose(1, 0, 2)
        flat.append(np.ascontiguousarray(x).reshape(-1))
    vs = []
    for n, k in VECS:
        vs.append(I[n].reshape(k, 128).T)
    C = np.zeros((128, NCF), np.float32)
    blk = np.kron(np.eye(2), np.ones((64, 64)))
    mats = {"ones1024": np.full((128, 128), 1 / 1024), "ones512": np.full((128, 128), 1 / 512),
            "ones128": np.full((128, 128), 1 / 128), "blk": blk, "blk64": blk / 64, "ident": np.eye(128)}
    for i, m in enumerate(MATS):
        C[:, i * 128:(i + 1) * 128] = mats[m]
    for i, e in enumerate(EPSCOLS):
        C[:, len(MATS) * 128 + i] = e
    s, t = np.meshgrid(np.arange(128), np.arange(128), indexing="ij")
    same = s // 64 == t // 64
    M = {"le": same & (s <= t), "lt": same & (s < t)}
    for i in range(6):
        m = 32 >> i
        M[f"g{i}"] = (s // (2 * m) == t // (2 * m)) & (s // m != t // m)
        m = 1 << i
        M[f"u{i}"] = (s // (2 * m) == t // (2 * m)) & (s // m < t // m)
        M[f"l{i}"] = M[f"u{i}"].T
    M["g6"] = s == t
    Cu = np.zeros((128, NCU), np.float32)
    for i, m in enumerate(MASKS):
        Cu[:, i * 128:(i + 1) * 128] = M[m]
    o = len(MASKS) * 128 + 256
    r = np.ones(528, np.float32)
    r[0] = 0
    r[16::64] = 0
    Cu[:, o:o + 528] = r
    r = np.ones(512, np.float32)
    r[0::64] = 0
    Cu[:, o + 528:] = r
    return {
        "wstream": np.concatenate(flat), "vecs": np.ascontiguousarray(np.concatenate(vs, 1)), "cf": C, "cu": Cu,
        "xT": np.ascontiguousarray(I["x"][0].T), "metaT": np.ascontiguousarray(I["meta_tokens"].T),
        "memT": np.ascontiguousarray(I["mem_2"][0].T),
        "pmix": np.ascontiguousarray(I["w_pool_mix"][0].transpose(1, 0, 2).reshape(128, 512)),
        "gup": np.ascontiguousarray(I["w_gate_up"][0]),
        "wau": np.ascontiguousarray(np.concatenate([I["w_up_2"][0], I["a_up_2"][0]], 0)),
        "gupg": np.ascontiguousarray(I["g_up_2"][0]),
    }


def kernel(**inputs):
    import numpy as _np
    import concourse.bacc as _bacc
    from concourse import mybir as _mybir
    from concourse.bass_utils import run_bass_kernel_spmd as _run

    nc = _bacc.Bacc("TRN2", target_bir_lowering=False, num_devices=1)
    arrays, args = {}, []
    for name, a in lay_out(inputs).items():
        arrays[f"in_{name}"] = a
        args.append(nc.dram_tensor(f"in_{name}", a.shape, _mybir.dt.from_np(a.dtype), kind="ExternalInput").ap())
    args.append(nc.dram_tensor("out_0", (1024, 512), _mybir.dt.float32, kind="ExternalOutput").ap())
    program(nc, *args)
    r = _run(nc, [arrays], core_ids=[0])
    return _np.ascontiguousarray(r.results[0]["out_0"].T).reshape(1, 512, 1024)
```

```python
import concourse.bass as bass
from concourse import mybir
from contextlib import ExitStack
import math

P = 128
UNIT = 2048
DECAY = math.exp(-0.5)
CSH = 26
LAG = 1

VECS = [("norm_mix", 8), ("pool_scale", 4), ("b_gate", 2), ("gla_norm", 4), ("norm_ffn", 8), ("norm_final", 8),
        ("mem_norm_g_2", 8), ("norm_gains_2", 48), ("mu_first_2", 14), ("conv_w_2", 124), ("conv_b_2", 4),
        ("conv_ln_g_2", 4), ("conv_ln_b_2", 4), ("w0_2", 4), ("a0_2", 4), ("k_k_2", 4), ("k_a_2", 4),
        ("r_k_2", 4), ("lnx_g_2", 4), ("lnx_b_2", 4)]
NV = sum(n for _, n in VECS)
EPSCOLS = [1e-6, 1e-5, 64e-5, 0.0]
MATS = ["ones1024", "ones512", "ones128", "blk", "blk64", "ident"]
NCF = len(MATS) * 128 + len(EPSCOLS) + 16
MASKS = [f"g{i}" for i in range(7)] + ["le", "lt"] + [f"u{i}" for i in range(6)]
RS0 = len(MASKS) * 128
NCU = RS0 + 528 + 512


def vcol(name):
    c = 0
    for n, k in VECS:
        if n == name:
            return c
        c += k
    raise KeyError(name)


P_ORDER = [12, 13, 4, 0, 8, 5, 1, 9, 6, 2, 10, 7, 3, 11]


def unit_list():
    u = []

    def t(tag, w, r0, nk, cols, width=128, kind="T"):
        u.append((tag, w, r0, nk, tuple(cols), width, kind))

    def pair(tag, w, c0, n, nk=8, r0=0):
        for i in range(n):
            t(tag, w, r0, nk, (c0 + 256 * i, c0 + 256 * i + 128))

    pair("a", "w_in", 0, 2)
    pair("k", "w_in", 768, 1)
    t("lr", "w_in", 0, 8, (2048,), 16)
    pair("q", "w_in", 512, 1)
    for i in range(2):
        t("v", "w_in", 0, 8, (1024 + 256 * i,), 256, "M")
    for i in range(2):
        t("po", "w_pool_out", 0, 4, [512 * i + 128 * j for j in range(4)])
    pair("r", "w_in", 1536, 2)
    pair("ga", "w_in", 2064, 4)
    pair("gb", "w_in", 3088, 4)
    for i in range(2):
        t("go", "w_gla_out", 0, 4, [512 * i + 128 * j for j in range(4)])
    pair("wo", "w_out", 0, 4)
    for g in range(4):
        pair("f1", "w_ff1", 1024 * g, 4)
        pair("f2", "w_ff2", 0, 4, 8, 1024 * g)
    for i in range(4):
        t("cv", "w_in_first_2", 0, 8, (128 * i, 512 + 128 * i))
    for i in range(7):
        t("p", "w_in_first_2", 0, 8, [1024 + 128 * P_ORDER[2 * i + j] for j in range(2)])
    pair("wo2", "w_out_2", 0, 4)
    pair("km", "wkv_2", 0, 4)
    for i in range(4):
        t("vm", "wkv_2", 0, 8, (1024 + 256 * i,), 256, "M")
    pair("wq", "wq_2", 0, 4)
    pair("xo", "wo_2", 0, 4)
    for g in range(3):
        nt = 8 if g < 2 else 6
        for i in range(nt):
            t("gu", "w_gu_2", 0, 8, (1024 * g + 128 * i, 2816 + 1024 * g + 128 * i))
        pair("dn", "w_down_2", 0, 4, nt, 1024 * g)
    return u


def unit_size(u):
    return u[3] * len(u[4]) * u[5]


class Tok:

    def __init__(self, eng):
        self.eng, self.used, self.sem, self.val = eng, False, None, 0


class Bank:
    def __init__(self, ap):
        self.ap, self.free = ap, []


def program(nc, wstream, vecs, cf, cu, xT, metaT, memT, pmix, gup, wau, gupg, out, x2s):
    f32, f32r, u8 = mybir.dt.float32, mybir.dt.float32r, mybir.dt.uint8
    ALU, ACT = mybir.AluOpType, mybir.ActivationFunctionType
    ctx = ExitStack()
    with ctx:
        def sb(name, shape, dt=f32):
            return ctx.enter_context(nc.sbuf_tensor(name, shape, dt))

        raw = [sb(f"raw{i}", [P, UNIT]) for i in range(2)]
        WH = [sb(f"wh{i}", [P, UNIT], f32r) for i in range(2)]
        WL = [sb(f"wl{i}", [P, UNIT], f32r) for i in range(2)]
        V = sb("vecs_sb", [P, NV + 8])
        C = sb("cf_sb", [P, NCF])
        U = sb("cu_sb", [P, NCU], u8)
        mh = sb("mh", [P, 8, 16])
        muh = sb("muh", [P, 8, 16], f32r)
        mul_ = sb("mul", [P, 8, 16], f32r)
        msq = sb("msq", [P, 2, 16])
        mrs = sb("mrs", [P, 16])
        lrs = sb("lrs", [16, 528])
        gup_sb = sb("gup_sb", [16, 256])
        khm = sb("khm", [16, 256])
        vmeta = sb("vmeta", [16, 512])
        sm = sb("sm", [P, 64])
        tn = sb("tn", [P, 64])
        dsm2 = sb("dsm2", [P, 16])
        cuts = [0, 8, 24, 34, 47, 55, 72]

        class Zone:

            def __init__(self, tag, dt):
                self.parts = []
                for a, b_ in zip(cuts, cuts[1:]):
                    pad = nc.sbuf_tensor(f"pad_{tag}{a}", [P, 512 * a], f32) if a else None
                    if pad:
                        pad.__enter__()
                    g = nc.sbuf_tensor(f"{tag}{a}", [P, 512 * (b_ - a)], dt)
                    self.parts.append((a * 512, b_ * 512, g.__enter__()))
                    g.__exit__(None, None, None)
                    if pad:
                        pad.__exit__(None, None, None)

            def __getitem__(self, key):
                a, b_ = key[1].start, key[1].stop
                for p0, p1, t in self.parts:
                    if p0 <= a and b_ <= p1:
                        return t[:, a - p0:b_ - p0]
                raise ValueError((a, b_))

        ZF, ZR = Zone("zf", f32), Zone("zr", f32r)
        sb("zone", [P, 512 * cuts[-1]])
        banks = [Bank(ctx.enter_context(nc.psum_tensor(f"ps{i}", [P, 512], f32))) for i in range(8)]

        def F(s, n=512):
            return ZF[:, s * 512:s * 512 + n]

        def R(s, n=512):
            return ZR[:, s * 512:s * 512 + n]

        def vec(name, i=0):
            c = vcol(name) + i
            return V[:, c:c + 1]

        def mat(name):
            i = MATS.index(name)
            return C[:, i * 128:(i + 1) * 128]

        def eps(i):
            return C[:, len(MATS) * 128 + i:len(MATS) * 128 + i + 1]

        def mask(name):
            i = MASKS.index(name)
            return U[:, i * 128:(i + 1) * 128]

        def mask4(name):
            return mask(name).unsqueeze(1).to_broadcast([P, 4, 128])

        RS528 = U[:, RS0:RS0 + 528]
        RS512 = U[:, RS0 + 528:NCU]

        names = ["pe", "act", "dve", "pool", "sp"]
        Q = {n: [] for n in names}
        esem = {n: ctx.enter_context(nc.semaphore(f"s_{n}")) for n in names[:4]}
        dsem, dcount = {}, {}

        def flat(x):
            for y in x:
                if y is None:
                    continue
                if isinstance(y, (list, tuple)):
                    yield from flat(y)
                else:
                    yield y

        def op(eng, fn, *after):
            after = list(flat(after))
            for t in after:
                t.used = True
            tok = Tok(eng)
            Q[eng].append((after, fn, tok))
            return tok

        def pe(fn, *a):
            return op("pe", fn, *a)

        def act(fn, *a):
            return op("act", fn, *a)

        def dve(fn, *a):
            return op("dve", fn, *a)

        def pool(fn, *a):
            return op("pool", fn, *a)

        def dma(sem, dst, src, *after):
            if sem not in dsem:
                dsem[sem] = ctx.enter_context(nc.semaphore(f"d_{sem}"))
                dcount[sem] = 0
            dcount[sem] += 16
            tok = op("sp", lambda e: e.dma_start(dst, src), *after)
            tok.eng, tok.sem, tok.val = "dma", dsem[sem], dcount[sem]
            return tok

        def A(out_, in_, fn, *after, scale=1.0, bias=0.0):
            return act(lambda e: e.activation(out_, in_, fn, bias=bias, scale=scale), *after)

        def copyA(out_, in_, *after, scale=1.0):
            return act(lambda e: e.activation(out_, in_, ACT.Copy, scale=scale), *after)

        def TT(out_, a, b, o, *after, eng="dve"):
            return op(eng, lambda e: e.tensor_tensor(out_, a, b, o), *after)

        def TS(out_, a, s1, o1, *after, s2=None, o2=None, eng="dve"):
            if o2 is None:
                return op(eng, lambda e: e.tensor_scalar(out_, a, s1, None, o1), *after)
            return op(eng, lambda e: e.tensor_scalar(out_, a, s1, s2, o1, o2), *after)

        def STT(out_, a, s, b, o1, o2, *after, eng="dve"):
            return op(eng, lambda e: e.scalar_tensor_tensor(out=out_, in0=a, scalar=s, in1=b, op0=o1, op1=o2), *after)

        def RCP(out_, a, *after):
            return dve(lambda e: e.reciprocal(out_, a), *after)

        def MM(out_, l, r, *after, start=True, stop=True):
            return pe(lambda e: e.matmul(out_, l, r, start=start, stop=stop), *after)

        def TR(out_, in_, idn, *after):
            return pe(lambda e: e.transpose(out_, in_, idn), *after)

        def rb(ap):
            return ap.bitcast(f32)

        def split(hi, lo, src, *after, eng="dve"):
            a = copyA(hi, src, *after)
            return [a, TT(lo, src, rb(hi), ALU.subtract, a, eng=eng)]

        def split_scaled(hi, lo, src, s, *after):
            a = copyA(hi, src, *after, scale=s)
            return [a, STT(lo, src, s, rb(hi), ALU.mult, ALU.subtract, a)]

        DB, MB = banks[:3], banks[3:]
        EPSV = EPSCOLS

        def powr(o_, *after):
            w = o_.shape[1]
            e_ = C[0:o_.shape[0], len(MATS) * 128 + len(EPSCOLS):len(MATS) * 128 + len(EPSCOLS) + w]
            return TT(o_, o_, e_, ALU.pow, TCF, *after, eng="pool")

        def spread(dst, o_, t, nt, free, pool_=None, rows=128):
            pool_ = DB if pool_ is None else pool_
            b = acq(pool_)
            for i in range(nt):
                t2 = MM(b.ap[:, i * 128:i * 128 + rows], o_[:, i:i + 1].to_broadcast([rows, 128]),
                        mat("ident")[0:rows, 0:rows], t, b.free)
            x = copyA(dst, b.ap[:, 0:(nt - 1) * 128 + rows], t2, free)
            rel(pool_, b, x)
            return x

        def acq(pool_):
            return pool_.pop(0)

        def rel(pool_, b, *toks):
            b.free = list(flat(toks))
            pool_.append(b)

        units = unit_list()
        offs, o = [], 0
        for u in units:
            offs.append(o)
            o += unit_size(u) * P
        wd, ws, wdone = {}, {}, {}
        nxt = [0]

        def wdma(n):
            if n >= len(units) or n in wd:
                return
            sz = unit_size(units[n])
            src = wstream[offs[n]:offs[n] + P * sz].rearrange("(p n) -> p n", n=sz)
            wd[n] = dma(f"w{n % 2}", raw[n % 2][:, 0:sz], src, ws.get(n - 2))

        def wsplit(n):
            if n >= len(units) or n in ws:
                return
            sz = unit_size(units[n])
            cuts = [(0, sz)] if sz <= 1024 else [(0, 1024), (1024, sz)]
            toks = []
            for a, b in cuts:
                h, l, r_ = WH[n % 2][:, a:b], WL[n % 2][:, a:b], raw[n % 2][:, a:b]
                t = copyA(h, r_, wd[n], wdone.get(n - 2))
                toks.append([t, TT(l, r_, rb(h), ALU.subtract, t, wdone.get(n - 2))])
            ws[n] = toks

        def wunit(tag):
            n = nxt[0]
            nxt[0] += 1
            assert units[n][0] == tag, (units[n], tag)
            wdma(n)
            wdma(n + 1)
            wsplit(n)
            wsplit(n + 1)
            wdma(n + 2)
            return n, units[n], WH[n % 2], WL[n % 2]

        bgs = []

        rate = [1]
        pace = {}

        def step_bg(n=None, mid=False):
            for g_ in list(bgs):
                r_ = pace.get(g_, rate[0])
                for _ in range(n if n is not None else r_ // 2 if mid else r_ - r_ // 2):
                    try:
                        next(g_)
                    except StopIteration:
                        bgs.remove(g_)
                        break

        def drain_bg(*gs):
            while any(g_ in bgs for g_ in gs) if gs else bgs:
                step_bg(1)

        def tile_T(unit, j, xs, N, evac, meta=None):
            n, u, wh, wl = unit
            nk, w = u[3], u[5]
            b = acq(DB)
            mb = acq(DB) if meta else None
            last = None
            for k in range(nk):
                c = (j * nk + k) * w
                lh, ll = wh[:, c:c + w], wl[:, c:c + w]
                xh, xl, xt = xs[k]
                wt = ws[n][min(c // 1024, len(ws[n]) - 1)]

                def go(e, lh=lh, ll=ll, xh=xh, xl=xl, k=k):
                    e.matmul(b.ap[0:w, 0:N], lh, xh, start=(k == 0), stop=False)
                    e.matmul(b.ap[0:w, 0:N], lh, xl, start=False, stop=False)
                    return e.matmul(b.ap[0:w, 0:N], ll, xh, start=False, stop=(k == nk - 1))
                last = pe(go, wt, xt, b.free if k == 0 else None)
                if k == nk // 2 - 1:
                    step_bg(mid=True)
            if meta:
                for k in range(nk):
                    c = (j * nk + k) * w
                    lh, ll = wh[:, c:c + w], wl[:, c:c + w]
                    xh, xl, xt = meta[k]

                    def go(e, lh=lh, ll=ll, xh=xh, xl=xl, k=k):
                        e.matmul(mb.ap[0:w, 0:16], lh, xh, start=(k == 0), stop=False)
                        e.matmul(mb.ap[0:w, 0:16], lh, xl, start=False, stop=False)
                        return e.matmul(mb.ap[0:w, 0:16], ll, xh, start=False, stop=(k == nk - 1))
                    last = pe(go, xt, mb.free if k == 0 else None)
            wdone[n] = last
            if meta:
                t, tm = evac(b.ap[0:w, 0:N], mb.ap[0:w, 0:16], last)
                rel(DB, b, t)
                rel(DB, mb, tm)
            else:
                rel(DB, b, evac(b.ap[0:w, 0:N], last))
            step_bg()
            return last

        def ko_step(unit, bs_, k, x, N):
            n, u, wh, wl = unit
            nk, w = u[3], u[5]
            xh, xl, xt = x
            for j in range(2):
                c = (j * nk + k) * w
                lh, ll = wh[:, c:c + w], wl[:, c:c + w]
                wt = ws[n][min(c // 1024, len(ws[n]) - 1)]

                def go(e, lh=lh, ll=ll, b=bs_[j]):
                    e.matmul(b.ap[0:w, 0:N], lh, xh, start=(k == 0), stop=False)
                    e.matmul(b.ap[0:w, 0:N], lh, xl, start=False, stop=False)
                    return e.matmul(b.ap[0:w, 0:N], ll, xh, start=False, stop=(k == nk - 1))
                last = pe(go, wt, xt, bs_[j].free if k == 0 else None)
            wdone[n] = last
            return last

        def pair_ko(unit, xs, N, meta=None):
            n, u, wh, wl = unit
            nk, w = u[3], u[5]
            bs_ = [acq(DB), acq(DB)]
            for k in range(nk):
                last = ko_step(unit, bs_, k, xs[k], N)
            mbs = []
            for j in range(2 if meta else 0):
                mb = acq(MB)
                mbs.append(mb)
                for k in range(nk):
                    c = (j * nk + k) * w
                    lh, ll = wh[:, c:c + w], wl[:, c:c + w]
                    xh, xl, xt = meta[k]

                    def go(e, lh=lh, ll=ll, xh=xh, xl=xl, k=k, mb=mb):
                        e.matmul(mb.ap[0:w, 0:16], lh, xh, start=(k == 0), stop=False)
                        e.matmul(mb.ap[0:w, 0:16], lh, xl, start=False, stop=False)
                        return e.matmul(mb.ap[0:w, 0:16], ll, xh, start=False, stop=(k == nk - 1))
                    last = pe(go, xt, mb.free if k == 0 else None)
            wdone[n] = last

            def fin(evs):
                for j in range(2):
                    if meta:
                        x, y = evs[j](bs_[j].ap[0:w, 0:N], mbs[j].ap[0:w, 0:16], last)
                        rel(MB, mbs[j], y)
                    else:
                        x = evs[j](bs_[j].ap[0:w, 0:N], last)
                    rel(DB, bs_[j], x)
                    step_bg()
                return last
            return fin

        def tile_M(unit, xs, t0, tn, evac):
            n, u, wh, wl = unit
            nk = u[3]
            b = acq(DB)
            for k in range(nk):
                rh, rl = wh[:, k * 256:k * 256 + 256], wl[:, k * 256:k * 256 + 256]
                xh, xl, xt = xs[k]
                xh, xl = xh[:, t0:t0 + tn], xl[:, t0:t0 + tn]
                wt = ws[n][min(k * 256 // 1024, len(ws[n]) - 1)]

                def go(e, rh=rh, rl=rl, xh=xh, xl=xl, k=k):
                    e.matmul(b.ap[0:tn, 0:256], xh, rh, start=(k == 0), stop=False)
                    e.matmul(b.ap[0:tn, 0:256], xh, rl, start=False, stop=False)
                    return e.matmul(b.ap[0:tn, 0:256], xl, rh, start=False, stop=(k == nk - 1))
                last = pe(go, wt, xt, b.free if k == 0 else None)
            wdone[n] = last
            rel(DB, b, evac(b.ap[0:tn, 0:256], last))
            step_bg()

        class Stat:

            def __init__(self, acc, tmps, N=512, free=None):
                self.acc, self.tmps, self.N, self.n, self.t = acc, tmps, N, 0, free
                self.tt = [free] * max(1, len(tmps))

            def add(self, src, *after, scale=1.0):
                if self.n == 0:
                    self.t = A(self.acc, src, ACT.Square, self.t, *after, scale=scale)
                    r_ = self.t
                else:
                    i = self.n % len(self.tmps)
                    tmp = self.tmps[i]
                    r_ = A(tmp, src, ACT.Square, self.tt[i], *after, scale=scale)
                    self.t = TT(self.acc, self.acc, tmp, ALU.add, r_, self.t, eng="pool")
                    self.tt[i] = self.t
                self.n += 1
                return r_

            def cols(self, c, *after, e_=0, m="ones1024", pool_=DB, rows=128, add=True):
                nt = max(1, self.N // 128)
                b = acq(pool_)
                for i in range(nt):
                    t = MM(b.ap[0:rows, i:i + 1], self.acc[:, i * 128:i * 128 + rows], mat(m)[:, 0:1], self.t, b.free,
                           TCF)
                self.done = t
                o_ = tn[0:rows, c:c + nt]
                x = TS(o_, b.ap[0:rows, 0:nt], EPSV[e_] if add else 0.0, ALU.add, t, *after)
                rel(pool_, b, x)
                return o_, (powr(o_, x) if add else x)

            def rstd(self, dst, c, e_=0, free=None, pool_=DB, after=None):
                o_, t = self.cols(c, after, e_=e_, pool_=pool_)
                self.rc, self.rt = o_, t
                return spread(dst, o_, t, self.N // 128, free, pool_=pool_)

        TV = dma("v", V[:, 0:NV], vecs)
        xv = xT.rearrange("(k p) t -> p k t", p=P)
        hx = [dma("x0", F(0), xv[:, 0, :])]
        wdma(0)
        for k in range(1, 8):
            hx.append(dma(f"x{k}", F(k), xv[:, k, :]))
        tm_ = dma("mh", mh[:, :, :], metaT.rearrange("(k p) t -> p k t", p=P))
        wdma(1)
        TCF = dma("cf", C[:, :], cf)
        cu_raw = F(55, NCU)
        tcu_raw = dma("cu", cu_raw, cu)
        pmx = F(54)
        tpm = dma("pm", pmx, pmix)
        tgu = dma("gu", gup_sb[:, :], gup)

        ACC, TMP, RSTD, TMP2 = F(66), F(67), F(68), F(69)

        st = Stat(ACC, [TMP, TMP2])
        stm = Stat(msq[:, 0, :], [msq[:, 1, :]], 16)
        xs, ms = [], []
        for k in range(8):
            t = split_scaled(R(8 + k), R(16 + k), F(k), vec("norm_mix", k), hx[k], TV)
            xs.append((R(8 + k), R(16 + k), t))
            if k == 0:
                wsplit(0)
        for k in range(8):
            t = split_scaled(muh[:, k, :], mul_[:, k, :], mh[:, k, :], vec("norm_mix", k), tm_, TV)
            ms.append((muh[:, k, :], mul_[:, k, :], t))
        for k in range(8):
            st.add(F(k), hx[k])
            stm.add(mh[:, k, :], tm_)

        def a_ap(i):
            return F(34, 2112)[:, i * 528:(i + 1) * 528]

        ta = [None] * 4

        def ev_a(i):
            def ev(p, pm, t):
                x = TT(a_ap(i)[:, 16:528], p, RSTD, ALU.mult, t, trs)
                y = TT(a_ap(i)[:, 0:16], pm, mrs[:, :], ALU.mult, t, trm)
                ta[i] = [x, y]
                return x, y
            return ev
        fin = pair_ko(wunit("a"), xs, 512, ms)
        trs = st.rstd(RSTD, 0)
        rc4, trc = st.rc, [st.rt]
        rcm, tm2 = stm.cols(4, rows=16)
        trc.append(tm2)
        trm = spread(mrs[:, :], rcm, tm2, 1, None, rows=16)
        fin([ev_a(0), ev_a(1)])
        un = wunit("a")
        for j in range(2):
            tile_T(un, j, xs, 512, ev_a(2 + j), ms)

        TCU = dve(lambda e: e.tensor_copy(U[:, :], cu_raw), tcu_raw)
        pooled = [None] * 4

        def bg_pool():
            for gi in range(4):
                src, tk = a_ap(gi), ta[gi]
                cur, width = src, 1
                for s in range(gi + 1):
                    n0 = 2 * width - 1
                    dst = F(47, 528) if s % 2 == 0 else ZF[:, 47 * 512 + 528:47 * 512 + 1056]
                    tk = TT(dst[:, n0:528], cur[:, n0:528], cur[:, n0 - width:528 - width], ALU.add, tk,
                            pooled[gi - 1] if gi and s == 0 else None)
                    cur, width = dst, 2 * width
                pooled[gi] = STT(F(43 + gi), cur[:, 16:528], 1.0 / width, src[:, 16:528], ALU.mult, ALU.subtract, tk)
                yield

        xdone = [x[2] for x in xs] + [trs]
        bgp = bg_pool()
        bgs.append(bgp)

        def k_ap(i):
            return F(24, 1056)[:, i * 528:(i + 1) * 528]

        tk_ = [None] * 2
        un = wunit("k")
        for j in range(2):
            def ev(p, pm, t, i=j):
                x = TT(k_ap(i)[:, 16:528], p, RSTD, ALU.mult, t, trs)
                y = TT(k_ap(i)[:, 0:16], pm, mrs[:, :], ALU.mult, t, trm)
                tk_[i] = [x, y]
                return x, y
            tile_T(un, j, xs, 512, ev, ms)
        un = wunit("lr")
        tlr = []

        def ev(p, pm, t):
            x = TT(lrs[:, 16:528], p, RSTD[0:16, :], ALU.mult, t, trs)
            y = TT(lrs[:, 0:16], pm, mrs[0:16, :], ALU.mult, t, trm)
            tlr.extend([x, y])
            return x, y
        tile_T(un, 0, xs, 512, ev, ms)
        un = wunit("q")
        tq = [None] * 2
        for j in range(2):
            def ev(p, t, i=j):
                tq[i] = STT(F(27 + i), p, 0.125, RSTD, ALU.mult, ALU.mult, t, trs)
                return tq[i]
            tile_T(un, j, xs, 512, ev)
        tv = [[] for _ in range(5)]
        state = {}

        def b_ap(i):
            return F(51, 1056)[:, i * 528:(i + 1) * 528]

        def bg_gla():
            tb = []
            Dm = [F(55 + i) for i in range(2)]
            parts = []
            for i in range(2):
                for n0, n1 in ((16, 528), (0, 16)):
                    w = n1 - n0
                    if w == 16:
                        xx, yy = sm[:, 32 * i:32 * i + 16], sm[:, 32 * i + 16:32 * i + 32]
                    else:
                        xx, yy = F([57, 62][i]), F([58, 63][i])
                    bk = acq(MB)
                    t = MM(bk.ap[:, 0:w], gup_sb[:, i * 128:(i + 1) * 128], lrs[:, n0:n1], tlr, tgu, bk.free)
                    a1 = A(xx, bk.ap[:, 0:w], ACT.Abs, t, TCU, bias=vec("b_gate", i))
                    m1 = TS(yy, bk.ap[:, 0:w], vec("b_gate", i), ALU.add, a1, TCU, s2=0.0, o2=ALU.min)
                    rel(MB, bk, m1, a1)
                    parts.append([i, n0, n1, xx, yy, a1, m1])
                yield
            for p_ in parts:
                p_[5] = A(p_[3], p_[3], ACT.Exp, p_[5], scale=-1.0)
            for p_ in parts:
                p_[5] = A(p_[3], p_[3], ACT.Ln, p_[5], bias=1.0)
            yield
            for i in range(2):
                ts = [TT(b_ap(i)[:, p_[1]:p_[2]], p_[4], p_[3], ALU.subtract, p_[5], p_[6]) for p_ in parts if p_[0] == i]
                tb.append(dve(lambda e, i=i: e.tensor_tensor_scan(
                    ZF[:, 59 * 512 + i * 528:59 * 512 + (i + 1) * 528], RS528, b_ap(i), 0.0, ALU.mult, ALU.add), ts, TCU))
                yield

            def bs(i, n0=0, n1=528):
                return ZF[:, 59 * 512 + i * 528 + n0:59 * 512 + i * 528 + n1]
            tsc = [dve(lambda e, i=i: e.memset(F(62 + i), 0.0), TCU, tb) for i in range(4)]
            prevm = None
            for l in range(7):
                if l < 6:
                    m = 32 >> l
                    fk = []
                    for i in range(2):
                        v3 = bs(i, 16, 528).rearrange("p (a b) -> p a b", b=2 * m)
                        ref = v3[:, :, m - 1:m].to_broadcast([P, 256 // m, 2 * m])
                        d3 = Dm[i].rearrange("p (a b) -> p a b", b=2 * m)
                        t = TT(d3, v3, ref, ALU.subtract, tb, state.get(("f", i)))
                        t = A(Dm[i], Dm[i], ACT.Abs, t)
                        t = A(Dm[i], Dm[i], ACT.Exp, t, scale=-1.0 / 16)
                        t1 = TT(F(57 + i), Dm[i], k_ap(i)[:, 16:528], ALU.mult, t, tk_[i], prevm, tb, eng="pool")
                        t2 = TT(F(51 + i), Dm[i], F(27 + i), ALU.mult, t, tq[i], prevm, tb)
                        state[("f", i)] = [t1, t2]
                        fk += [t1, t2]
                        yield
                    yield
                    kk = [F(57 + i) for i in range(2)]
                    qq = [F(51 + i) for i in range(2)]
                else:
                    kk = [k_ap(i)[:, 16:528] for i in range(2)]
                    qq = [F(27 + i) for i in range(2)]
                    fk = []
                for tp_ in range(2):
                    bb_ = [acq(MB), acq(MB)]
                    for par in range(2):
                        lo = 64 * par
                        for tl_ in range(2):
                            cs = slice((2 * tp_ + tl_) * 128, (2 * tp_ + tl_ + 1) * 128)
                            for i in range(2):
                                t = MM(bb_[par].ap[:, (2 * tl_ + i) * 128:(2 * tl_ + i + 1) * 128], kk[i][lo:lo + 64, cs],
                                       qq[i][lo:lo + 64, cs], fk, bb_[par].free, tk_, tq)
                        z = 2 * tp_ + par
                        sc3 = F(62 + z).rearrange("p (a b) -> p a b", b=128)
                        ps3 = bb_[par].ap[:, :].rearrange("p (a b) -> p a b", b=128)
                        tsc[z] = dve(lambda e, sc3=sc3, ps3=ps3, l=l: e.copy_predicated(sc3, mask4(f"g{l}"), ps3),
                                     t, tsc[z], TCU)
                        rel(MB, bb_[par], tsc[z])
                        prevm = t
                    yield
            tqh, tkh = [], []
            for i in range(2):
                t = A(Dm[i], bs(i, 16, 528), ACT.Exp, state[("f", i)], scale=1.0 / 16)
                t1 = TT(F(51 + i), Dm[i], F(27 + i), ALU.mult, t, prevm)
                v3 = bs(i, 16, 528).rearrange("p (a b) -> p a b", b=64)
                t2 = copyA(sm[:, 8 * i:8 * i + 8].unsqueeze(2), v3[:, :, 63:64], t)
                t2 = A(sm[:, 8 * i:8 * i + 8], sm[:, 8 * i:8 * i + 8], ACT.Exp, t2, scale=1.0 / 16)
                tqh.append(t1)
                d3 = Dm[i].rearrange("p (a b) -> p a b", b=64)
                ref = v3[:, :, 63:64].to_broadcast([P, 8, 64])
                t = TT(d3, v3, ref, ALU.subtract, t1, t2)
                t = A(Dm[i], Dm[i], ACT.Exp, t, scale=-1.0 / 16)
                t = TT(F(57 + i), Dm[i], k_ap(i)[:, 16:528], ALU.mult, t, prevm)
                tm1 = TT(sm[:, 32 + 16 * i:48 + 16 * i], bs(i, 0, 16), bs(i, 15, 16).to_broadcast([P, 16]), ALU.subtract, tb)
                tm1 = A(sm[:, 32 + 16 * i:48 + 16 * i], sm[:, 32 + 16 * i:48 + 16 * i], ACT.Exp, tm1, scale=-1.0 / 16)
                tm1 = TT(sm[:, 32 + 16 * i:48 + 16 * i], sm[:, 32 + 16 * i:48 + 16 * i], k_ap(i)[:, 0:16], ALU.mult, tm1)
                tkh.append([t, tm1, t2])
                yield
            tkt = []
            for i in range(2):
                b = acq(MB)
                for tt in range(4):
                    t = TR(b.ap[:, tt * 128:(tt + 1) * 128], F(57 + i)[:, tt * 128:(tt + 1) * 128], mat("ident"), tkh[i], b.free)
                x = copyA(F(59 + i), b.ap[:, :], t, tkh, tqh)
                rel(MB, b, x)
                b = acq(MB)
                t = TR(b.ap[0:16, 0:128], sm[:, 32 + 16 * i:48 + 16 * i], mat("ident"), b.free)
                y = copyA(khm[:, i * 128:(i + 1) * 128], b.ap[0:16, 0:128], t)
                rel(MB, b, y)
                tkt.append([x, y])
                yield

            while len(tv[4]) < 2:
                yield
            def S(c, i):
                z = (c * 2 + i) * 128
                if z < 512 + 512:
                    return ZF[:, 55 * 512 + z:55 * 512 + z + 128]
                return ZF[:, 24 * 512 + (z - 1024):24 * 512 + (z - 1024) + 128]
            b = acq(MB)
            for i in range(2):
                for hh in range(2):
                    h = 2 * i + hh
                    t = MM(b.ap[hh * 64:hh * 64 + 64, i * 128:(i + 1) * 128], khm[:, h * 64:h * 64 + 64],
                           vmeta[:, h * 128:(h + 1) * 128], tkt, tv[4], b.free)
            tS = {}
            for i in range(2):
                tS[(0, i)] = copyA(S(0, i), b.ap[:, i * 128:(i + 1) * 128], t, tkt, tkh, tqh)
            rel(MB, b, tS[(0, 0)], tS[(0, 1)])
            yield
            for c in range(7):
                b = acq(MB)
                r0 = 64 * (c % 2)
                for i in range(2):
                    for hh in range(2):
                        h = 2 * i + hh
                        t = MM(b.ap[hh * 64:hh * 64 + 64, i * 128:(i + 1) * 128],
                               F(59 + i)[r0:r0 + 64, (c // 2) * 128 + hh * 64:(c // 2) * 128 + hh * 64 + 64],
                               F(29 + c // 2)[r0:r0 + 64, h * 128:(h + 1) * 128], tkt, tv, b.free)
                for i in range(2):
                    tS[(c + 1, i)] = STT(S(c + 1, i), S(c, i), sm[:, 8 * i + c:8 * i + c + 1], b.ap[:, i * 128:(i + 1) * 128],
                                         ALU.mult, ALU.add, t, tS[(c, i)], tkh, prevm, tkt)
                rel(MB, b, tS[(c + 1, 0)], tS[(c + 1, 1)])
                yield
            to = []
            OS = [57, 58, 27, 28]
            state["OS"] = OS
            for h in range(4):
                i, hh = h // 2, h % 2
                b = acq(MB)
                for tt in range(4):
                    cs = slice(tt * 128, (tt + 1) * 128)
                    MM(b.ap[:, cs], F(29 + tt)[:, h * 128:(h + 1) * 128], F(62 + 2 * (tt // 2) + hh)[:, (2 * (tt % 2) + i) * 128:(2 * (tt % 2) + i + 1) * 128],
                       tsc, tv, b.free, stop=False)
                    for c in (2 * tt, 2 * tt + 1):
                        t = MM(b.ap[:, c * 64:(c + 1) * 64], S(c, i)[hh * 64:hh * 64 + 64, :],
                               F(51 + i)[hh * 64:hh * 64 + 64, c * 64:(c + 1) * 64], tS[(c, i)], tqh, start=False,
                               stop=(c % 2 == 1))
                x = copyA(F(OS[h]), b.ap[:, :], t, tkt, tqh)
                rel(MB, b, x)
                to.append(x)
                tlast_o = t
                yield
            state["tlast_o"] = tlast_o
            ys = []
            for h in range(4):
                so = Stat(F(59), [], free=[tlast_o, ys])
                so.add(F(OS[h]), to[h])
                yield
                o_, s = so.cols(8 + 4 * h, m="ones128", pool_=MB)
                yield
                s = spread(F(60), o_, s, 4, ys, pool_=MB)
                y = STT(F(OS[h]), F(OS[h]), vec("gla_norm", h), F(60), ALU.mult, ALU.mult, s)
                ys.append(y)
                yield
            state["o"] = ys
            state["done_gla"] = ys

        bgg = bg_gla()
        bgs.append(bgg)

        for uu in range(2):
            un = wunit("v")
            for i in range(4):
                def ev(p, t, i=i, uu=uu):
                    x = TS(F(29 + i)[:, 256 * uu:256 * uu + 256], p, rc4[:, i:i + 1], ALU.mult, t, trc)
                    tv[i].append(x)
                    return x
                tile_M(un, xs, 128 * i, 128, ev)

            def ev(p, t, uu=uu):
                x = TS(vmeta[:, 256 * uu:256 * uu + 256], p, rcm, ALU.mult, t, trc)
                tv[4].append(x)
                return x
            tile_M(un, ms, 0, 16, ev)

        drain_bg(bgp)
        mixed = []
        for gi in range(4):
            b = acq(DB)
            t = MM(b.ap[:, :], pmx[:, gi * 128:(gi + 1) * 128], F(43 + gi), pooled, tpm, b.free)
            t1 = split_scaled(R(34 + gi), R(39 + gi), b.ap[:, :], vec("pool_scale", gi), t, ta, pooled)
            rel(DB, b, t1)
            mixed.append((R(34 + gi), R(39 + gi), t1))
            tmix = t

        rate[0] = 2

        tya = [None] * 8
        for uu in range(2):
            un = wunit("po")
            for j in range(4):
                i = 4 * uu + j

                def ev(p, t, i=i):
                    tya[i] = copyA(F(43 + i), p, t, tmix, pooled)
                    return tya[i]
                tpo = tile_T(un, j, mixed, 512, ev)
        tsr = [None] * 4
        for uu in range(2):
            un = wunit("r")
            for j in range(2):
                i = 2 * uu + j

                def ev(p, t, i=i):
                    x = TT(F(34 + i), p, RSTD, ALU.mult, t, trs, tpo)
                    s = A(F(39 + i), F(34 + i), ACT.Sigmoid, x, tpo)
                    tsr[i] = TT(F(34 + i), F(34 + i), F(39 + i), ALU.mult, s, x, eng="pool")
                    return x
                tile_T(un, j, xs, 512, ev)
        rate[0] = 2
        tg = [None, None]
        for uu in range(4):
            un = wunit("ga")
            for j in range(2):
                i = 2 * uu + j

                def ev(p, t, i=i):
                    T = TMP if i % 2 == 0 else TMP2
                    x = TT(T, p, RSTD, ALU.mult, t, trs, tg[i % 2])
                    s = A(T, T, ACT.Sigmoid, x)
                    tya[i] = TT(F(43 + i), F(43 + i), T, ALU.mult, s, tya[i], eng="pool")
                    tg[i % 2] = tya[i]
                    return x
                tile_T(un, j, xs, 512, ev)
        GB = list(range(8))
        tgb = [None] * 8
        for uu in range(4):
            un = wunit("gb")
            for j in range(2):
                i = 2 * uu + j

                def ev(p, t, i=i):
                    x = TT(F(GB[i]), p, RSTD, ALU.mult, t, trs, xdone)
                    tgb[i] = A(F(GB[i]), F(GB[i]), ACT.Sigmoid, x)
                    return x
                last_gb = tile_T(un, j, xs, 512, ev)
        drain_bg()
        OS = state["OS"]
        os_ = []
        for h in range(4):
            t = TT(F(OS[h]), F(OS[h]), F(34 + h), ALU.mult, state["o"][h], tsr[h])
            t = split(R(62 + h), R(29 + h), F(OS[h]), t, state["tlast_o"])
            os_.append((R(62 + h), R(29 + h), t))
        m_ = []
        xr = [None] * 8
        for uu in range(2):
            un = wunit("go")
            for j in range(4):
                i = 4 * uu + j

                def ev(p, t, i=i):
                    x = TT(F(GB[i]), p, F(GB[i]), ALU.mult, t, tgb[i])
                    y = TT(F(GB[i]), F(GB[i]), F(43 + i), ALU.add, x, tya[i], eng="pool")
                    s = split(R(8 + i), R(16 + i), F(GB[i]), y, last_gb)
                    m_.append((R(8 + i), R(16 + i), s))
                    xr[i] = dma(f"x{i}", F(i), xv[:, i, :], s, y)
                    return x
                last_go = tile_T(un, j, os_, 512, ev)
        st = Stat(ACC, [TMP, TMP2], free=[trs, tg, trc])
        u2, th = [], [None] * 8
        for uu in range(4):
            un = wunit("wo")
            for j in range(2):
                i = 2 * uu + j

                def ev(p, t, i=i):
                    x = TT(F(i), F(i), p, ALU.add, t, xr[i])
                    th[i] = [x, st.add(F(i), x)]
                    s = split_scaled(R(24 + i), R(32 + i), F(i), vec("norm_ffn", i), x, last_go, m_[7][2], tgb, tsr)
                    th[i].append(s)
                    u2.append((R(24 + i), R(32 + i), s))
                    return x
                last_wo = tile_T(un, j, m_, 512, ev)
        hid_free = last_go
        gfg = V[:, NV:NV + 8]
        tgf = TT(gfg, V[:, vcol("norm_final"):vcol("norm_final") + 8], V[:, vcol("norm_gains_2"):vcol("norm_gains_2") + 8],
                 ALU.mult, TV)
        fst = [None, None]
        xs2 = []
        for g_ in range(4):
            hs = []

            def ev_f(i, hid_free=hid_free, hs=hs):
                def ev(p, t):
                    T, T2 = F(56 + i % 2), F(58 + i % 2)
                    x = STT(T, p, 0.0, RSTD, ALU.max, ALU.mult, t, trs, fst[i % 2], tgb)
                    y = A(T2, T, ACT.Square, x, fst[i % 2])
                    s = split(R(40 + i), R(48 + i), T2, y, hid_free, eng="pool")
                    fst[i % 2] = s
                    hs.append((R(40 + i), R(48 + i), s))
                    return x
                return ev
            for uu in range(4):
                un = wunit("f1")
                if g_ == 0 and uu == 0:
                    fin = pair_ko(un, u2, 512)
                    trs = st.rstd(RSTD, 0, free=[tgb])
                    stA = Stat(F(60), [F(61), F(62)], free=[last_go, last_wo])
                    stB = Stat(ACC, [TMP, TMP2], free=st.done)
                    fin([ev_f(0), ev_f(1)])
                    continue
                for j in range(2):
                    tile_T(un, j, u2, 512, ev_f(2 * uu + j))
            for uu in range(4):
                un = wunit("f2")
                for j in range(2):
                    i = 2 * uu + j

                    def ev(p, t, i=i, g_=g_):
                        x = TT(F(i), F(i), p, ALU.add, t, th[i])
                        th[i] = [x]
                        if g_ == 3:
                            th[i].append(stA.add(F(i), x))
                            th[i].append(stB.add(F(i), x, scale=vec("norm_final", i)))
                            s = split_scaled(R(8 + i), R(16 + i), F(i), gfg[:, i:i + 1], x, tgf, last_wo)
                            th[i].append(s)
                            xs2.append((R(8 + i), R(16 + i), s))
                        return x
                    hid_free = tile_T(un, j, hs, 512, ev)
        fin = pair_ko(wunit("cv"), xs2, 512)
        RA = F(63)
        cA, t1 = stA.cols(24)
        tra = spread(RA, cA, t1, 4, [hid_free])
        cB, t2 = stB.cols(28, add=False)
        x = TT(cB, cB, cA, ALU.mult, t1, t2)
        x = TT(cB, cB, cA, ALU.mult, x)
        x = TS(cB, cB, 1e-6, ALU.add, x)
        x = powr(cB, x)
        x = TT(cB, cB, cA, ALU.mult, x)
        trs = spread(RSTD, cB, x, 4, [fst])
        x2v = x2s.rearrange("(k p) t -> p k t", p=P)
        tx, tsp = [], []

        ZC = [ZF[:, 47 * 512 + 542 * i:47 * 512 + 542 * (i + 1)] for i in range(4)]
        tcz = [dve(lambda e, i=i: e.memset(ZC[i][:, 0:30], 0.0), hid_free) for i in range(4)]
        thc, tcu = [None] * 4, [None] * 4
        cgf = [fst, fst]

        def ev_cv(i, j):
            def ev(p, t):
                if j == 0:
                    tcu[i] = TT(ZC[i][:, 30:542], p, RSTD, ALU.mult, t, trs, hid_free)
                    return tcu[i]
                T = F(56 + i % 2)
                x = TT(T, p, RSTD, ALU.mult, t, trs, cgf[i % 2])
                s = A(T, T, ACT.Sigmoid, x)
                thc[i] = TT(ZC[i][:, 30:542], ZC[i][:, 30:542], T, ALU.mult, s, tcu[i], tcz[i])
                cgf[i % 2] = thc[i]
                return x
            return ev
        fin([ev_cv(0, 0), ev_cv(0, 1)])
        for i in range(8):
            tx.append(STT(F(i), F(i), vec("norm_final", i), RA, ALU.mult, ALU.mult, tra, th[i]))
            tsp.append(dma("x2o", x2v[:, i, :], F(i), tx[i]))
        CO = [F(52), F(53), F(54), F(55)]
        cvres = []

        tc = [None] * 4
        CP = F(58)
        pt = [None, None]

        def taps(i, t0, t1, dst, eng):
            while thc[i] is None:
                yield
            t = None
            tmps, tf = [F(59), F(60)], [fst, fst]
            for tap in range(t0, t1):
                w = V[:, vcol("conv_w_2") + tap * 4 + i:vcol("conv_w_2") + tap * 4 + i + 1]
                src = ZC[i][:, tap:tap + 512]
                if tap == 0:
                    t = TS(dst, src, w, ALU.mult, thc[i], tcz, hid_free, s2=vec("conv_b_2", i), o2=ALU.add, eng=eng)
                elif tap == t0:
                    t = TS(dst, src, w, ALU.mult, thc[i], tcz, hid_free, fst, eng=eng)
                elif eng == "dve":
                    t = STT(dst, src, w, dst, ALU.mult, ALU.add, t)
                else:
                    z = tap % 2
                    m = copyA(tmps[z], src, thc[i], tcz, tf[z], pt[z], scale=w)
                    t = TT(dst, dst, tmps[z], ALU.add, m, t, eng="pool")
                    tf[z] = pt[z] = t
                yield
            return t

        def bg_conv_pool():
            tc[0] = yield from taps(0, 0, 31, CO[0], "pool")
            state["cp"] = yield from taps(3, 31 - CSH, 31, CP, "pool")

        def bg_conv():
            for i in range(1, 4):
                it = taps(i, 0, 31 if i < 3 else 31 - CSH, CO[i], "dve")
                tc[i] = yield from it
            while "cp" not in state:
                yield
            tc[3] = TT(CO[3], CO[3], CP, ALU.add, tc[3], state["cp"])
            yield
            b = acq(MB)
            for i in range(4):
                t = MM(b.ap[:, :], mat("ones512"), CO[i], tc[i], b.free, start=(i == 0), stop=(i == 3))
            mt = []
            for i in range(4):
                mt.append(TT(CO[i], CO[i], b.ap[:, :], ALU.subtract, t))
            rel(MB, b, mt)
            yield
            so = Stat(F(58), [F(59), F(60)], free=[hid_free, trs, tx, tc[3]])
            for i in range(4):
                so.add(CO[i], mt[i])
                yield
            o_, s = so.cols(52, e_=1, m="ones512", pool_=MB)
            yield
            s = spread(F(61), o_, s, 4, [trs], pool_=MB)
            yield
            for i in range(4):
                x = STT(CO[i], CO[i], vec("conv_ln_g_2", i), F(61), ALU.mult, ALU.mult, s, mt[i])
                x = TS(CO[i], CO[i], vec("conv_ln_b_2", i), ALU.add, x)
                T = F(56 + i % 2)
                g_ = A(T, CO[i], ACT.Sigmoid, x, cgf[i % 2])
                x = TT(F(47 + i), CO[i], T, ALU.mult, g_, x, tc)
                cgf[i % 2] = x
                cvres.append(x)
                yield
            D["cvdone"] = cvres
            state["conv"] = True

        D = {}
        cv1, cv2 = bg_conv(), bg_conv_pool()
        bgs += [cv1, cv2]
        pace[cv1], pace[cv2] = 4, 3
        rate[0] = 2
        for i in range(1, 4):
            un = wunit("cv")
            tile_T(un, 0, xs2, 512, ev_cv(i, 0))
            last_cv = tile_T(un, 1, xs2, 512, ev_cv(i, 1))

        wau_sb, gupg_sb = F(40), F(41)
        tw1 = dma("wau", wau_sb, wau, hid_free)
        tw2 = dma("gupg", gupg_sb, gupg, hid_free)
        ZB = [ZF[:, 42 * 512 + 520 * i:42 * 512 + 520 * i + 513] for i in range(2)]
        zfree = [dve(lambda e, i=i: e.memset(ZB[i][:, 0:1], 0.0), hid_free) for i in range(2)]
        zc = [0]
        slot_of = {**{i: 24 + i for i in range(12)}, 12: 36, 13: 37}
        hv = V[:, NV:NV + 8]
        thv = [TS(hv[:, 0:4], V[:, vcol("w0_2"):vcol("w0_2") + 4], 0.5, ALU.mult, xs2[7][2]),
               TS(hv[:, 4:8], V[:, vcol("a0_2"):vcol("a0_2") + 4], 0.5, ALU.mult, xs2[7][2])]
        tp = {}


        RO = [24, 25, 26, 27]
        KS = [28, 29, 30, 31]
        VS = [32, 33, 34, 35]

        def v4(x):
            return x.rearrange("p (a b) -> p a b", b=128)

        def c64(x):
            return x.rearrange("p (a b) -> p a b", b=64)

        def lag():
            for _ in range(LAG):
                if "pdone" not in D:
                    yield

        def bg_prep():
            sg, at, TC, TD, kkv, kp = F(38), F(39), F(65), F(66), F(67), F(69)
            Pp, nB = F(0), F(1)
            pv = [trs, tx, tsp]
            for hp in range(4):
                while not all(f in tp for f in (12, 13, hp, 4 + hp, 8 + hp)):
                    yield
                r_, Kk, v_ = F(RO[hp]), F(KS[hp]), F(VS[hp])
                yield
                yield from lag()
                z_ = hp % 2
                nBt, Kt, Vt, Pt = F(3 + z_), F(5 + z_), F([7, 52][z_]), F([2, 59][z_])
                dsm = dsm2[:, 8 * z_:8 * z_ + 8]
                b = acq(MB)
                t = MM(b.ap[:, :], wau_sb[0:64, hp * 128:(hp + 1) * 128], F(36)[0:64, :], tp[12], tw1, b.free)
                x = A(sg, b.ap[:, :], ACT.Tanh, t, pv, thv, bias=hv[:, hp:hp + 1], scale=0.5)
                rel(MB, b, x)
                b = acq(MB)
                t = MM(b.ap[:, :], wau_sb[64:128, hp * 128:(hp + 1) * 128], F(36)[64:128, :], b.free)
                y = A(at, b.ap[:, :], ACT.Tanh, t, pv, thv, bias=hv[:, 4 + hp:5 + hp], scale=0.5)
                rel(MB, b, y)
                x = TS(sg, sg, 0.5, ALU.mult, x, s2=0.5, o2=ALU.add)
                y = TS(at, at, 0.5, ALU.mult, y, s2=0.5, o2=ALU.add)
                yield
                tb = dve(lambda e: e.tensor_tensor_scan(TC, RS512, sg, 0.0, ALU.mult, ALU.add), x, TCU, pv)
                b3 = c64(TC)
                mid = b3[:, :, 31:32]
                while hp >= 2 and ("fin", hp - 2) not in D:
                    yield
                fz = D.get(("fin", hp - 2))
                z = TT(dsm.unsqueeze(2), b3[:, :, 63:64], mid, ALU.subtract, tb, fz)
                z = TT(dsm[:, 0:7].unsqueeze(2), dsm[:, 0:7].unsqueeze(2), b3[:, 1:8, 31:32], ALU.add, z)
                tD = A(dsm, dsm, ACT.Exp, z, scale=-DECAY)
                tdd = TT(c64(TD), b3, mid.to_broadcast([P, 8, 64]), ALU.subtract, tb, pv)
                yield
                q1 = TS(kkv, Kk, vec("k_k_2", hp), ALU.mult, tp[4 + hp], pv)
                q2 = A(TC, kkv, ACT.Square, q1, z, tdd)
                yield
                yield from lag()
                b = acq(MB)
                hs2 = c64(mat("blk"))[:, :, 0:1]
                for tt in range(4):
                    t = MM(b.ap[:, 2 * tt:2 * tt + 2], TC[:, tt * 128:(tt + 1) * 128], hs2, q2, b.free)
                nc_ = tn[:, 36:44]
                q3 = TS(nc_, b.ap[:, 0:8], 1e-24, ALU.max, t)
                rel(MB, b, q3)
                q3 = powr(nc_, q3)
                yield
                yield from lag()
                b = acq(MB)
                for tt in range(4):
                    for hh in range(2):
                        t = MM(b.ap[64 * hh:64 * hh + 64, tt * 128:(tt + 1) * 128],
                               nc_[:, 2 * tt + hh:2 * tt + hh + 1].to_broadcast([P, 64]), mat("ident"), q3, b.free)
                tkk = TT(kkv, kkv, b.ap[:, :], ALU.mult, t, q1)
                rel(MB, b, tkk)
                q4 = TS(TC, at, 1.0, ALU.subtract, y, t, s2=vec("k_a_2", hp), o2=ALU.mult)
                tkp = STT(kp, TC, 1.0, Kk, ALU.add, ALU.mult, q4, pv)
                yield
                q5 = STT(TC, r_, vec("r_k_2", hp), kp, ALU.mult, ALU.mult, tkp, tp[hp])
                yield
                yield from lag()
                b = acq(MB)
                t = MM(b.ap[:, :], mat("blk"), TC, q5, b.free)
                bon, tbon = b, t
                b = acq(MB)
                for tt in range(4):
                    cs = slice(tt * 128, (tt + 1) * 128)
                    t = TR(b.ap[:, cs], v_[:, cs], mat("ident"), tp[8 + hp], b.free)
                while z_ and "conv" not in state:
                    yield
                tVt = copyA(Vt, b.ap[:, :], t, fz, pv, D.get("cvdone") if z_ else None)
                rel(MB, b, tVt)
                tBV = TT(v_, bon.ap[:, :], v_, ALU.mult, tbon, t, tp[8 + hp])
                rel(MB, bon, tBV)
                yield
                while hp >= 1 and not (("prodq", hp - 1, 0) in D and ("prodq", hp - 1, 1) in D):
                    yield
                pf = [D.get((f, hp - 1, hh)) for f in ("prod", "prodq") for hh in range(2)] if hp else [pv]
                e1 = A(Pp, TD, ACT.Exp, tdd, pf, scale=-DECAY)
                tro = TT(r_, r_, Pp, ALU.mult, e1, tp[hp], q5)
                e2 = A(Kk, TD, ACT.Exp, tdd, tkp, q1, scale=DECAY)
                e3 = TT(nB, kkv, at, ALU.mult, tkk, y, pf)
                tnB = STT(nB, nB, -1.0, Kk, ALU.mult, ALU.mult, e3, e2)
                tKk = TT(Kk, kp, Kk, ALU.mult, tkp, tnB, e2)
                yield
                e4 = TT(TD, TD, sg, ALU.subtract, e1, e2, tdd)
                e4 = A(TD, TD, ACT.Exp, e4, scale=-DECAY)
                tP = TT(Pp, kkv, TD, ALU.mult, e4, tro, tkk)
                yield
                yield from lag()
                ttr = []
                for src, dst, tk in ((nB, nBt, tnB), (Kk, Kt, tKk), (Pp, Pt, tP)):
                    b = acq(MB)
                    for tt in range(4):
                        cs = slice(tt * 128, (tt + 1) * 128)
                        t = TR(b.ap[:, cs], src[:, cs], mat("ident"), tk, b.free)
                    x = copyA(dst, b.ap[:, :], t, fz, pf)
                    rel(MB, b, x)
                    ttr.append(x)
                    yield
                pv = [tP, tnB, tKk, tro, tBV, q5, tkp, e4, tD]
                D[("prep", hp)] = {"in": [tro, tP, tnB, tKk, tVt] + ttr, "nBt": nBt, "Pt": Pt, "Kt": Kt, "Vt": Vt, "ro": r_,
                                   "K": Kk, "dsm": dsm, "tD": tD, "BV": v_, "tBV": tBV}

        def bg_head(z_, hh):
            r0 = 64 * hh
            AT, AA, Z, T = [F(i) for i in [(10, 11, 12, 13), (14, 15, 16, 17), (18, 19, 20, 21),
                                           (22, 23, 68, 70)][2 * z_ + hh]]
            X1 = AT
            PX = F([71, 58][z_])[:, 256 * hh:256 * hh + 256]
            Pp, nB = F(0), F(1)
            RT = F([62, 63, 53, 54][2 * z_ + hh])
            QT = F([64, 46, 55, 56][2 * z_ + hh])
            PK = F([45, 44, 57, 61][2 * z_ + hh])
            GH = PK
            last = [None]

            def turn(src, tk):
                b = acq(MB)
                for tt in range(4):
                    cs = slice(tt * 128, (tt + 1) * 128)
                    t = TR(b.ap[:, cs], src[:, cs], mat("ident"), tk, b.free)
                return b, t

            def mul(l, r, *tk):
                b = acq(MB)
                for tt in range(4):
                    cs = slice(tt * 128, (tt + 1) * 128)
                    t = MM(b.ap[:, cs], l[:, cs], r[:, cs], tk, b.free)
                return b, t
            for hp in (z_, z_ + 2):
                while ("prep", hp) not in D or (hp >= 2 and ("fin", hp - 2) not in D) or "pdone" not in D:
                    yield
                while z_ and "conv" not in state:
                    yield
                d = D[("prep", hp)]
                ro, Kk, Vt, Pt, din = d["ro"], d["K"], d["Vt"], d["Pt"], d["in"]
                fz = [D.get(("fin", hp - 2)), last, D["pdone"], cvres if z_ else None]

                def prod(lhs, rhs):
                    b = acq(MB)
                    for tt in range(4):
                        cs = slice(tt * 128, (tt + 1) * 128)
                        t = MM(b.ap[:, cs], lhs[r0:r0 + 64, cs], rhs[r0:r0 + 64, cs], b.free, din)
                    return b, t

                b, t = prod(nB, Pp)
                tAT = TT(v4(AT), v4(b.ap[:, :]), mask4("lt"), ALU.mult, t, fz)
                rel(MB, b, tAT)
                tZ = TT(v4(Z), v4(AT), mask4("u0"), ALU.mult, tAT, fz)
                tZ = TT(v4(Z), v4(Z), mask4("g6"), ALU.add, tZ)
                yield
                b, t = prod(Kk, Pp)
                tPK = TT(v4(PK), v4(b.ap[:, :]), mask4("lt"), ALU.mult, t, fz)
                rel(MB, b, tPK)
                D[("prod", hp, hh)] = [t]
                b, t = turn(AT, tAT)
                tAA = copyA(AA, b.ap[:, :], t, fz)
                tATf = t
                rel(MB, b, tAA)
                yield
                b, t = turn(Z, tZ)
                tT = copyA(T, b.ap[:, :], t, fz)
                rel(MB, b, tT)
                yield

                def side(n):
                    if n == 1:
                        b, t = prod(Kk, ro)
                        out_ = TT(v4(RT), v4(b.ap[:, :]), mask4("le"), ALU.mult, t, fz)
                    elif n == 2:
                        b, t = prod(nB, ro)
                        D[("prodq", hp, hh)] = [t]
                        out_ = TT(v4(QT), v4(b.ap[:, :]), mask4("le"), ALU.mult, t, fz)
                    else:
                        b = acq(MB)
                        for tt in range(4):
                            t = MM(b.ap[:, tt * 64:(tt + 1) * 64], PK[:, tt * 128:(tt + 1) * 128],
                                   Vt[:, tt * 128 + r0:tt * 128 + r0 + 64], tPK, b.free, din)
                        out_ = copyA(PX, b.ap[:, 0:256], t, fz)
                    rel(MB, b, out_)
                    return out_
                sd = {}
                tx0 = [tATf, tZ]
                for l in range(1, 6):
                    b, t = mul(AA, Z, tAA, tZ)
                    tX1 = TT(v4(X1), v4(b.ap[:, :]), mask4(f"u{l}"), ALU.mult, t, tx0)
                    rel(MB, b, tX1)
                    if l < 4:
                        sd[l] = side(l)
                    yield
                    b, t = mul(T, X1, tX1, tT)
                    tZ = TT(Z, Z, b.ap[:, :], ALU.add, t, tZ)
                    rel(MB, b, tZ)
                    yield
                    if l < 5:
                        b, t = turn(Z, tZ)
                        tT = copyA(T, b.ap[:, :], t)
                        rel(MB, b, tT)
                        yield
                b = acq(MB)
                for tt in range(4):
                    cs = slice(tt * 128, (tt + 1) * 128)
                    MM(b.ap[:, tt * 128:tt * 128 + 64], Z[:, cs], Pt[:, tt * 128 + r0:tt * 128 + r0 + 64], tZ, b.free)
                    t = MM(b.ap[:, tt * 128 + 64:tt * 128 + 128], Z[:, cs], PX[:, tt * 64:(tt + 1) * 64], sd[3])
                tGH = copyA(GH, b.ap[:, :], t, fz)
                rel(MB, b, tGH)
                last = [t, tGH]
                D[("head", hp, hh)] = dict(GH=GH, tGH=tGH, QT=QT, tQT=sd[2], RT=RT, tRT=sd[1])
                yield

        yr = [None] * 4

        def bg_fin():
            Y1, M2, ND, SS = F(8), F(9), F(42), F(43)
            prev = None
            for hp in range(4):
                while ("head", hp, 0) not in D or ("head", hp, 1) not in D:
                    yield
                d = D[("prep", hp)]
                res = [D[("head", hp, 0)], D[("head", hp, 1)]]
                nBt, Kt, Vt, ro, dsm, tD = d["nBt"], d["Kt"], d["Vt"], d["ro"], d["dsm"], d["tD"]
                fz = [D["pdone"], prev]
                b = acq(MB)
                for hh in range(2):
                    r0 = 64 * hh
                    for tt in range(4):
                        cs = slice(tt * 128, (tt + 1) * 128)
                        t = MM(b.ap[r0:r0 + 64, cs], res[hh]["GH"][:, tt * 128:tt * 128 + 64], res[hh]["QT"][:, cs],
                               res[hh]["tGH"], res[hh]["tQT"], b.free)
                tY1 = TT(Y1, b.ap[:, :], ro, ALU.add, t, d["in"], fz)
                rel(MB, b, tY1)
                yield
                bb_ = [acq(MB), acq(MB)]
                tl = []
                for par in range(2):
                    c0 = 64 * par
                    n2 = 4 - par
                    for hh in range(2):
                        r0 = 64 * hh
                        for a_ in range(n2):
                            t = MM(bb_[par].ap[r0:r0 + 64, a_ * 64:(a_ + 1) * 64],
                                   res[hh]["GH"][c0:c0 + 64, a_ * 128:a_ * 128 + 64],
                                   nBt[c0:c0 + 64, a_ * 128 + r0:a_ * 128 + r0 + 64], bb_[par].free, d["in"])
                    one = []
                    for hh in range(2):
                        r0 = 64 * hh
                        idn = mat("ident")[r0:r0 + 64, r0:r0 + 64].unsqueeze(1).to_broadcast([64, n2, 64])
                        mv = M2[r0:r0 + 64, :].rearrange("p (a two b) -> p two a b", two=2, b=64)[:, par, 0:n2, :]
                        one.append(TT(mv, c64(bb_[par].ap[r0:r0 + 64, 0:64 * n2]), idn, ALU.add, t, fz))
                    rel(MB, bb_[par], one)
                    tl += one
                yield
                bb_ = [acq(MB), acq(MB)]
                tN = []
                for par in range(2):
                    c0 = 64 * par
                    n2 = 4 - par
                    for hh in range(2):
                        r0 = 64 * hh
                        for a_ in range(n2):
                            kc = slice(a_ * 128 + r0, a_ * 128 + r0 + 64)
                            o_ = bb_[par].ap[r0:r0 + 64, a_ * 64:(a_ + 1) * 64]
                            MM(o_, Kt[c0:c0 + 64, kc], Vt[c0:c0 + 64, kc], bb_[par].free, stop=False)
                            t = MM(o_, nBt[c0:c0 + 64, kc], res[hh]["GH"][c0:c0 + 64, a_ * 128 + 64:a_ * 128 + 128],
                                   start=False)
                    nv = ND.rearrange("p (a two b) -> p two a b", two=2, b=64)[:, par, 0:n2, :]
                    dv = dsm.rearrange("p (a two) -> p two a", two=2)[:, par, 0:n2].unsqueeze(2).to_broadcast([P, n2, 64])
                    x = TT(nv, c64(bb_[par].ap[:, 0:64 * n2]), dv, ALU.mult, t, tD, fz)
                    rel(MB, bb_[par], x)
                    tN.append(x)
                yield
                tS = dve(lambda e: e.memset(SS[:, 0:64], 0.0), fz)
                tS = [tS, dve(lambda e: e.tensor_copy(SS[:, 64:128], ND[:, 0:64]), tN, fz)]
                for c in range(1, 7):
                    b = acq(MB)
                    for hh in range(2):
                        r0 = 64 * hh
                        t = MM(b.ap[r0:r0 + 64, 0:64], M2[r0:r0 + 64, c * 64:(c + 1) * 64],
                               SS[r0:r0 + 64, c * 64:(c + 1) * 64], b.free, tS, tl)
                    tS = STT(SS[:, (c + 1) * 64:(c + 2) * 64], b.ap[:, 0:64], dsm[:, c:c + 1],
                             ND[:, c * 64:(c + 1) * 64], ALU.mult, ALU.add, t, tD, tN)
                    rel(MB, b, tS)
                    yield
                b = acq(MB)
                for hh in range(2):
                    r0 = 64 * hh
                    for tt in range(4):
                        cs = slice(tt * 128, (tt + 1) * 128)
                        o_ = b.ap[r0:r0 + 64, cs]
                        MM(o_, Vt[:, tt * 128 + r0:tt * 128 + r0 + 64], res[hh]["RT"][:, cs], b.free, res[hh]["tRT"],
                           stop=False)
                        MM(o_, res[hh]["GH"][:, tt * 128 + 64:tt * 128 + 128], res[hh]["QT"][:, cs], start=False, stop=False)
                        for c in (2 * tt, 2 * tt + 1):
                            t = MM(b.ap[r0:r0 + 64, c * 64:(c + 1) * 64], SS[r0:r0 + 64, c * 64:(c + 1) * 64],
                                   Y1[r0:r0 + 64, c * 64:(c + 1) * 64], tS, tY1, start=False, stop=(c % 2 == 1))
                yy, T1 = M2, ND
                ty = copyA(yy, b.ap[:, :], t)
                rel(MB, b, ty)
                D[("fin", hp)] = [t, tS]
                yield
                b = acq(MB)
                t = MM(b.ap[:, :], mat("blk64"), yy, ty, b.free)
                t1_ = TT(yy, yy, b.ap[:, :], ALU.subtract, t)
                rel(MB, b, t1_)
                t2_ = A(T1, yy, ACT.Square, t1_, tS)
                yield
                b = acq(MB)
                hs2 = c64(mat("blk64"))[:, :, 0:1]
                for tt in range(4):
                    t = MM(b.ap[:, 2 * tt:2 * tt + 2], T1[:, tt * 128:(tt + 1) * 128], hs2, t2_, b.free)
                gc = tn[:, 44:52]
                x = TS(gc, b.ap[:, 0:8], 64e-5, ALU.add, t)
                rel(MB, b, x)
                x = powr(gc, x)
                t4_ = TS(yy, yy, vec("lnx_g_2", hp), ALU.mult, t1_, t2_)
                yield
                b = acq(MB)
                for tt in range(4):
                    for hh in range(2):
                        t = MM(b.ap[64 * hh:64 * hh + 64, tt * 128:(tt + 1) * 128],
                               gc[:, 2 * tt + hh:2 * tt + hh + 1].to_broadcast([P, 64]), mat("ident"), x, b.free)
                t4_ = TT(yy, yy, b.ap[:, :], ALU.mult, t4_, t)
                rel(MB, b, t4_)
                b = acq(MB)
                t = MM(b.ap[:, :], gupg_sb[:, hp * 128:(hp + 1) * 128], F(37), tp[13], tw2, b.free)
                t4_ = STT(yy, yy, vec("lnx_b_2", hp), d["BV"], ALU.add, ALU.add, t4_, d["tBV"])
                t4_ = TT(yy, yy, b.ap[:, :], ALU.mult, t4_, t)
                rel(MB, b, t4_)
                s = split(R(RO[hp]), R(KS[hp]), yy, t4_, tY1, d["in"])
                yr[hp] = (R(RO[hp]), R(KS[hp]), s)
                prev = [t, s, t4_]
                yield

        prep = bg_prep()
        pace[prep] = 2
        bgs += [prep, bg_head(0, 0), bg_head(0, 1), bg_head(1, 0), bg_head(1, 1), bg_fin()]
        oi = 0
        for uu in range(7):
            un = wunit("p")
            for j in range(2):
                f = P_ORDER[oi]
                oi += 1

                def ev(p, t, f=f):
                    z = ZB[zc[0] % 2]
                    zi = zc[0] % 2
                    zc[0] += 1
                    dd = F(45 + zi)
                    x = TT(z[:, 1:513], p, RSTD, ALU.mult, t, trs, zfree[zi])
                    y = TT(dd, z[:, 0:512], z[:, 1:513], ALU.subtract, x, zfree[zi], hid_free, eng="pool")
                    w = STT(F(slot_of[f]), dd, vec("mu_first_2", f), z[:, 1:513], ALU.mult, ALU.add, y, x, hid_free)
                    zfree[zi] = [w, y]
                    if f == 12:
                        w = A(F(36)[0:64, :], F(36)[0:64, :], ACT.Tanh, w)
                    if f == 13:
                        w = A(F(37), F(37), ACT.Sigmoid, w)
                    tp[f] = w
                    return x
                last_p = tile_T(un, j, xs2, 512, ev)
        D["pdone"] = [last_p, zfree]
        rate[0] = 2

        cat = [None] * 8
        W2 = {}

        def bg_out():
            while not all(f in D for f in (("head", 2, 0), ("head", 2, 1), ("prep", 3))):
                yield
            hd = [D[("head", 2, 0)]["tGH"], D[("head", 2, 1)]["tGH"], D[("prep", 3)]["in"]]
            ch = [R(16), R(17), R(60), R(38)]
            W2["u"] = wunit("wo2")
            for i in range(4):
                cat[i] = (ch[i], R(47 + i), split(ch[i], R(47 + i), F(47 + i), cvres[i], hd))
                if i % 2:
                    yield
            bb_ = [acq(DB), acq(DB)]
            W2["b"] = bb_
            while ("head", 3, 0) not in D:
                yield
            for k in range(8):
                while k >= 4 and yr[k - 4] is None:
                    yield
                if k >= 4:
                    cat[k] = yr[k - 4]
                    if k < 7:
                        yield
                        yield
                W2["t"] = ko_step(W2["u"], bb_, k, cat[k], 512)
                yield

        MB.append(DB.pop(0))
        bgs.append(bg_out())
        drain_bg()
        DB.append(MB.pop(0))
        allrw = [p_[2] for p_ in yr] + [D[("fin", 3)]]
        txr = [dma(f"x{i}", F(i), x2v[:, i, :], tsp, allrw) for i in range(8)]
        tx = list(txr)

        def residual(ys, yt, gi, tx, t, nxt_slots, nxt_g, wfree, stat_next, outp):
            for i in range(8):
                a = STT(ys[i], ys[i], vec("norm_gains_2", 8 * gi + i), RSTD, ALU.mult, ALU.mult, t, yt[i])
                tx[i] = TT(F(i), F(i), ys[i], ALU.add, a, tx[i], eng="pool" if i % 2 else "dve")
                q_ = stat_next.add(F(i), tx[i])
                yield
                hi, lo = nxt_slots[i]
                s = split_scaled(hi, lo, F(i), vec("norm_gains_2", 8 * nxt_g + i), tx[i], wfree)
                tx[i] = [tx[i], q_, s]
                outp.append((hi, lo, s))
                yield

        YS = [F(8 + i) for i in range(8)]
        stat = Stat(F(63), [F(64), F(65)], free=[allrw])
        yt = [None] * 8
        for uu in range(4):
            un = wunit("wo2") if uu else None
            for j in range(2):
                i = 2 * uu + j

                def ev(p, t, i=i):
                    x = copyA(YS[i], p, t, allrw)
                    yt[i] = [x, stat.add(YS[i], x)]
                    return x
                if uu:
                    last_o2 = tile_T(un, j, cat, 512, ev)
                else:
                    rel(DB, W2["b"][j], ev(W2["b"][j].ap[:, :], W2["t"]))
        mraw = F(42, 2048)
        tmr = dma("mem", mraw.rearrange("p (k t) -> p k t", t=256), memT.rearrange("(k p) t -> p k t", p=P), allrw)
        mst = Stat(F(39)[:, 0:256], [F(39)[:, 256:512]], 256, free=[allrw])
        mx = []
        mlo = [36, 37, 40, 41]
        for k in range(8):
            src = mraw[:, k * 256:(k + 1) * 256]
            ks = slice((k % 2) * 256, (k % 2) * 256 + 256)
            hi, lo = R(32 + k // 2)[:, ks], R(mlo[k // 2])[:, ks]
            s = split_scaled(hi, lo, src, vec("mem_norm_g_2", k), tmr, allrw)
            mst.add(src, tmr)
            mx.append((hi, lo, s))
        MR = F(38)[:, 0:256]
        km_ap = [F(47 + i // 2)[:, (i % 2) * 256:(i % 2) * 256 + 256] for i in range(8)]
        vsl = [51, 58, 59, 60]
        vm_ap = [[F(vsl[2 * mt + c // 2])[:, (c % 2) * 256:(c % 2) * 256 + 256] for c in range(4)] for mt in range(2)]
        fin = pair_ko(wunit("km"), mx, 256)
        trs = stat.rstd(RSTD, 0, free=[last_o2, last_p])
        tmrs = mst.rstd(MR, 8, free=[allrw, last_o2])
        mc, tmc = mst.rc, mst.rt
        tkm = [None] * 8

        def ev_km(i):
            def ev(p, t):
                tkm[i] = TT(km_ap[i], p, MR, ALU.mult, t, tmrs, last_o2)
                return tkm[i]
            return ev
        fin([ev_km(0), ev_km(1)])
        st3 = Stat(F(66), [F(67), F(69)], free=[allrw])
        xlo = [52, 53, 54, 55, 56, 57, 61, 62]

        xs3 = []
        bgr = residual(YS, yt, 1, tx, trs, [(R(16 + i), R(xlo[i])) for i in range(8)], 2,
                       [last_o2, allrw], st3, xs3)
        bgs.append(bgr)
        pace[bgr] = 1
        for uu in range(1, 4):
            un = wunit("km")
            for j in range(2):
                tile_T(un, j, mx, 256, ev_km(2 * uu + j))
        tvm = []
        for uu in range(4):
            un = wunit("vm")
            for mt in range(2):
                def ev(p, t, uu=uu, mt=mt):
                    x = TS(vm_ap[mt][uu], p, mc[:, mt:mt + 1], ALU.mult, t, tmc, last_o2)
                    tvm.append(x)
                    return x
                tile_M(un, mx, mt * 128, 128, ev)
        drain_bg(bgr)
        tqq = [None] * 8
        QS = YS

        ao = [None] * 8
        AD = {}

        def bg_att():
            prf = [None, None]
            ptfree = [None, None]

            def scores(h):
                z = h % 2
                tpr = []
                for tt in range(4):
                    b = acq(MB)
                    for d in range(2):
                        t = MM(b.ap[:, 0:256], QS[2 * h + d][:, tt * 128:(tt + 1) * 128], km_ap[2 * h + d],
                               tqq[2 * h + d], tkm, b.free, start=(d == 0), stop=(d == 1))
                    c = 16 * z + 4 * tt
                    nm, ssum = sm[:, c:c + 1], sm[:, c + 1:c + 2]
                    pr = F(24 + 2 * z + tt // 2)[:, (tt % 2) * 256:(tt % 2) * 256 + 256]
                    x = dve(lambda e, nm=nm, b=b: e.tensor_reduce(nm, b.ap[:, 0:256], mybir.AxisListType.X, ALU.max,
                                                                negate=True), t, prf[z], allrw)
                    y = act(lambda e, pr=pr, b=b, nm=nm, ssum=ssum: e.activation(
                        pr, b.ap[:, 0:256], ACT.Exp, bias=nm, scale=1.0, accum_out=ssum), x, prf[z], last_o2)
                    rel(MB, b, y)
                    w = RCP(ssum, ssum, y)
                    w = TS(pr, pr, ssum, ALU.mult, w, y)
                    tpr.append(w)
                    if tt % 2:
                        yield
                AD[h] = tpr
            for h in range(5):
                if h < 4:
                    while tqq[2 * h] is None or tqq[2 * h + 1] is None:
                        yield
                    yield from scores(h)
                g_ = h - 1
                if g_ < 0:
                    continue
                z = g_ % 2
                tpr = AD[g_]
                PT = [F(28 + 2 * z), F(29 + 2 * z)]
                tt_ = []
                for mt in range(2):
                    b = acq(MB)
                    for tt in range(4):
                        src = F(24 + 2 * z + tt // 2)[:, (tt % 2) * 256 + mt * 128:(tt % 2) * 256 + mt * 128 + 128]
                        t = TR(b.ap[:, tt * 128:(tt + 1) * 128], src, mat("ident"), tpr, b.free)
                    x = copyA(PT[mt], b.ap[:, :], t, ptfree[z], last_o2)
                    rel(MB, b, x)
                    tt_.append(x)
                prf[z] = [t]
                yield
                for d in range(2):
                    b = acq(MB)
                    for mt in range(2):
                        t = MM(b.ap[:, :], vm_ap[mt][g_][:, d * 128:(d + 1) * 128], PT[mt], tt_, tvm, b.free,
                               start=(mt == 0), stop=(mt == 1))
                    i = 2 * g_ + d
                    hi, lo = R(32 + i), R(40 + i if i < 7 else 63)
                    s = split(hi, lo, b.ap[:, :], t, tvm, tkm)
                    rel(MB, b, s)
                    ao[i] = (hi, lo, s)
                ptfree[z] = [t]
                AD["last"] = t
                yield
        bga = bg_att()
        bgs.append(bga)
        pace[bga] = 3
        trs3 = None

        def ev_q(i):
            def ev(p, t):
                tqq[i] = STT(QS[i], p, 1.0 / 16, RSTD, ALU.mult, ALU.mult, t, trs3, tx)
                return tqq[i]
            return ev
        fin = pair_ko(wunit("wq"), xs3, 512)
        trs3 = st3.rstd(RSTD, 4, free=[tx])
        fin([ev_q(0), ev_q(1)])
        rate[0] = 1
        for uu in range(1, 4):
            un = wunit("wq")
            for j in range(2):
                last_q = tile_T(un, j, xs3, 512, ev_q(2 * uu + j))
        drain_bg()
        last_att = AD["last"]
        stat = Stat(F(64), [F(65), F(66)], free=[last_att, trs3])
        yt = [None] * 8
        for uu in range(4):
            un = wunit("xo")
            for j in range(2):
                i = 2 * uu + j

                def ev(p, t, i=i):
                    x = copyA(YS[i], p, t, last_att)
                    yt[i] = [x, stat.add(YS[i], x)]
                    return x
                last_xo = tile_T(un, j, ao, 512, ev)
        st4 = Stat(F(67), [F(69), F(63)], free=[trs3, last_xo])
        trs = stat.rstd(RSTD, 12, free=[tqq])
        xs4 = []
        for _ in residual(YS, yt, 3, tx, trs, [(R(16 + i), R(24 + i)) for i in range(8)], 4, [last_xo], st4, xs4):
            pass
        fst = [None, None]
        dn_free = last_xo
        AC = [F(48 + i) for i in range(8)]
        tac = [None] * 8
        stat = Stat(F(60), [F(61), F(62)], free=[last_xo])
        trs4 = None
        for g_ in range(3):
            nt = 8 if g_ < 2 else 6
            hs = []

            def ev_g(i, j, dn_free=dn_free, hs=hs):
                T, T2 = F(56 + i % 2), F(58 + i % 2)

                def ev0(p, t):
                    x = TT(T, p, RSTD, ALU.mult, t, trs4, fst[i % 2], tx)
                    y = A(T2, T, ACT.Sigmoid, x, fst[i % 2])
                    y = TT(T, T, T2, ALU.mult, x, y, eng="pool")
                    fst[i % 2] = y
                    return x

                def ev1(p, t):
                    x = TT(T2, p, RSTD, ALU.mult, t, fst[i % 2])
                    y = TT(T, T, T2, ALU.mult, x, fst[i % 2], eng="pool")
                    s = split(R(32 + i), R(40 + i), T, y, dn_free, eng="pool")
                    fst[i % 2] = s
                    hs.append((R(32 + i), R(40 + i), s))
                    return x
                return ev1 if j else ev0
            for i in range(nt):
                un = wunit("gu")
                if g_ == 0 and i == 0:
                    fin = pair_ko(un, xs4, 512)
                    trs4 = st4.rstd(RSTD, 16, free=[tx])
                    fin([ev_g(0, 0), ev_g(0, 1)])
                    continue
                for j in range(2):
                    tile_T(un, j, xs4, 512, ev_g(i, j))
            for uu in range(4):
                un = wunit("dn")
                for j in range(2):
                    i = 2 * uu + j

                    def ev(p, t, i=i, g_=g_):
                        if g_ == 0:
                            x = copyA(AC[i], p, t, last_xo, tx)
                            tac[i] = x
                        else:
                            x = TT(AC[i], AC[i], p, ALU.add, t, tac[i])
                            tac[i] = x
                        if g_ == 2:
                            tac[i] = [x, stat.add(AC[i], x)]
                        return x
                    dn_free = tile_T(un, j, hs, 512, ev)
        t = stat.rstd(RSTD, 56, free=[fst])
        ov = out.rearrange("(k p) t -> p k t", p=P)
        outs = []
        for i in range(8):
            a = STT(AC[i], AC[i], vec("norm_gains_2", 40 + i), RSTD, ALU.mult, ALU.mult, t, tac[i])
            a = TT(F(i), F(i), AC[i], ALU.add, a, tx[i], eng="pool" if i % 2 else "dve")
            outs.append(dma("out", ov[:, i, :], F(i), a))
        op("sp", None, outs)

        for n in names[:4]:
            c = 0
            for after, fn, tok in Q[n]:
                if tok.used:
                    c += 1
                    tok.sem, tok.val = esem[n], c

        def run(eng, n):
            seen = {}
            for after, fn, tok in Q[n]:
                need = {}
                for t in after:
                    if n == "pe" and t.eng == "pe":
                        continue
                    k = t.sem.name
                    if t.val > need.get(k, (0, None))[0]:
                        need[k] = (t.val, t.sem)
                for k, (v, s) in need.items():
                    if v > seen.get(k, 0):
                        eng.wait_ge(s, v)
                        seen[k] = v
                if fn is None:
                    continue
                ins = fn(eng)
                if tok.eng == "dma":
                    ins.then_inc(tok.sem, 16)
                elif tok.used:
                    ins.then_inc(tok.sem, 1)

        block = ctx.enter_context(nc.Block())

        @block.sync
        def _(eng):
            run(eng, "sp")

        @block.tensor
        def _(eng):
            run(eng, "pe")

        @block.scalar
        def _(eng):
            run(eng, "act")

        @block.vector
        def _(eng):
            run(eng, "dve")

        @block.gpsimd
        def _(eng):
            run(eng, "pool")


def lay_out(inputs):
    import numpy as np
    I = {k: np.asarray(v) for k, v in inputs.items()}
    flat = []
    for tag, w, r0, nk, cols, width, kind in unit_list():
        W = I[w].reshape(I[w].shape[-2], I[w].shape[-1])[r0:r0 + nk * 128]
        if kind == "T":
            x = np.stack([W[:, c:c + width].reshape(nk, 128, width) for c in cols], 0)
            x = x.transpose(2, 0, 1, 3)
        else:
            x = W[:, cols[0]:cols[0] + width].reshape(nk, 128, width).transpose(1, 0, 2)
        flat.append(np.ascontiguousarray(x).reshape(-1))
    vs = []
    for n, k in VECS:
        vs.append(I[n].reshape(k, 128).T)
    C = np.zeros((128, NCF), np.float32)
    blk = np.kron(np.eye(2), np.ones((64, 64)))
    mats = {"ones1024": np.full((128, 128), 1 / 1024), "ones512": np.full((128, 128), 1 / 512),
            "ones128": np.full((128, 128), 1 / 128), "blk": blk, "blk64": blk / 64, "ident": np.eye(128)}
    for i, m in enumerate(MATS):
        C[:, i * 128:(i + 1) * 128] = mats[m]
    for i, e in enumerate(EPSCOLS):
        C[:, len(MATS) * 128 + i] = e
    C[:, len(MATS) * 128 + len(EPSCOLS):] = -0.5
    s, t = np.meshgrid(np.arange(128), np.arange(128), indexing="ij")
    same = s // 64 == t // 64
    M = {"le": same & (s <= t), "lt": same & (s < t)}
    for i in range(6):
        m = 32 >> i
        M[f"g{i}"] = (s // (2 * m) == t // (2 * m)) & (s // m != t // m)
        m = 1 << i
        M[f"u{i}"] = (s // (2 * m) == t // (2 * m)) & (s // m < t // m)
    M["g6"] = s == t
    Cu = np.zeros((128, NCU), np.float32)
    for i, m in enumerate(MASKS):
        Cu[:, i * 128:(i + 1) * 128] = M[m]
    o = RS0
    r = np.ones(528, np.float32)
    r[0] = 0
    r[16::64] = 0
    Cu[:, o:o + 528] = r
    r = np.ones(512, np.float32)
    r[0::64] = 0
    Cu[:, o + 528:] = r
    return {
        "wstream": np.concatenate(flat), "vecs": np.ascontiguousarray(np.concatenate(vs, 1)), "cf": C, "cu": Cu,
        "xT": np.ascontiguousarray(I["x"][0].T), "metaT": np.ascontiguousarray(I["meta_tokens"].T),
        "memT": np.ascontiguousarray(I["mem_2"][0].T),
        "pmix": np.ascontiguousarray(I["w_pool_mix"][0].transpose(1, 0, 2).reshape(128, 512)),
        "gup": np.ascontiguousarray(I["w_gate_up"][0]),
        "wau": np.ascontiguousarray(np.concatenate([I["w_up_2"][0], I["a_up_2"][0]], 0)),
        "gupg": np.ascontiguousarray(I["g_up_2"][0]),
    }


def kernel(**inputs):
    import numpy as _np
    import concourse.bacc as _bacc
    from concourse import mybir as _mybir
    from concourse.bass_utils import run_bass_kernel_spmd as _run

    nc = _bacc.Bacc("TRN2", target_bir_lowering=False, num_devices=1)
    arrays, args = {}, []
    for name, a in lay_out(inputs).items():
        arrays[f"in_{name}"] = a
        args.append(nc.dram_tensor(f"in_{name}", a.shape, _mybir.dt.from_np(a.dtype), kind="ExternalInput").ap())
    args.append(nc.dram_tensor("out_0", (1024, 512), _mybir.dt.float32, kind="ExternalOutput").ap())
    args.append(nc.dram_tensor("x2_scratch", (1024, 512), _mybir.dt.float32, kind="Internal").ap())
    program(nc, *args)
    r = _run(nc, [arrays], core_ids=[0])
    return _np.ascontiguousarray(r.results[0]["out_0"].T).reshape(1, 512, 1024)
```
